# Optimizing a Trainium2 kernel written in Bass

```python
import jax, jax.numpy as jnp
from jax import lax
import numpy as np

D_MODEL = 1024
BATCH = 1
SEQ = 1024
DEPTH = 2

CHUNK = 64
HEAD_DIM = 64
N_HEADS_A = 8
N_HEADS_B = 8
D_A = N_HEADS_A * HEAD_DIM
D_B = N_HEADS_B * HEAD_DIM
D_MIX = D_A + D_B
IN_COLS = 2 * D_A + 3 * D_B
GMLP_BLOCK = 128
ATT_LEFT_CHUNKS = 8
ATT_BAND = (ATT_LEFT_CHUNKS + 1) * CHUNK
REL_CLIP = 128
N_REL = 2 * REL_CLIP + 1
CONV_WIDTH = 31
D_CONV = D_MODEL
D_FF = ((-(-8 * D_MODEL // 3)) + 255) // 256 * 256
N_EVEN = (DEPTH + 1) // 2
N_ODD = DEPTH // 2
EPS = 1e-6
NEG_INF = -1e30

kernel_name = "hybrid_gmlp_relattn_conformerconv_encoder"

def _rmsnorm(x, g):
    xf = x.astype(jnp.float32)
    y = xf * lax.rsqrt(jnp.mean(xf * xf, axis=-1, keepdims=True) + EPS)
    return (y * g.astype(jnp.float32)).astype(x.dtype)

def _layernorm(x, g, b):
    xf = x.astype(jnp.float32)
    mu = jnp.mean(xf, axis=-1, keepdims=True)
    var = jnp.mean(jnp.square(xf - mu), axis=-1, keepdims=True)
    y = (xf - mu) * lax.rsqrt(var + EPS)
    return (y * g.astype(jnp.float32) + b.astype(jnp.float32)).astype(x.dtype)

def _mixer_a(u, v, ln_g, ln_b, w_s, b_s):
    bsz, seq, _ = u.shape
    nb = seq // GMLP_BLOCK
    u = jax.nn.gelu(u)
    v = _layernorm(jax.nn.gelu(v), ln_g, ln_b)
    v = v.reshape(bsz, nb, GMLP_BLOCK, N_HEADS_A, HEAD_DIM)
    pos_chunk = jnp.arange(GMLP_BLOCK) // CHUNK
    mask = (pos_chunk[None, :] <= pos_chunk[:, None]).astype(w_s.dtype)
    w = w_s * mask[None]
    gate = jnp.einsum('hij,bnjhd->bnihd', w, v) + b_s.T[None, None, :, :, None]
    return u * gate.reshape(bsz, seq, D_A)

def _mixer_b(q, k, v, rel_bias):
    bsz, seq, _ = q.shape
    nc = seq // CHUNK
    shp = (bsz, nc, CHUNK, N_HEADS_B, HEAD_DIM)
    q, k, v = q.reshape(shp), k.reshape(shp), v.reshape(shp)
    pad = ((0, 0), (ATT_LEFT_CHUNKS, 0), (0, 0), (0, 0), (0, 0))
    kp, vp = jnp.pad(k, pad), jnp.pad(v, pad)

    def band(t):
        return jnp.concatenate([t[:, w:w + nc] for w in range(ATT_LEFT_CHUNKS + 1)], axis=2)

    kb, vb = band(kp), band(vp)
    s = jnp.einsum('bnqhd,bnkhd->bhnqk', q, kb).astype(jnp.float32) * (HEAD_DIM ** -0.5)
    qi = jnp.arange(CHUNK)
    kj = jnp.arange(ATT_BAND)
    rel = ATT_LEFT_CHUNKS * CHUNK + qi[:, None] - kj[None, :]
    rel_idx = jnp.clip(rel, -REL_CLIP, REL_CLIP) + REL_CLIP
    bias = rel_bias[:, rel_idx].astype(jnp.float32)
    key_chunk = jnp.arange(nc)[:, None] - ATT_LEFT_CHUNKS + (kj // CHUNK)[None, :]
    valid = key_chunk >= 0
    s = jnp.where(valid[None, None, :, None, :], s + bias[None, :, None], NEG_INF)
    p = jax.nn.softmax(s, axis=-1).astype(vb.dtype)
    o = jnp.einsum('bhnqk,bnkhd->bnqhd', p, vb)
    return o.reshape(bsz, seq, D_B)

def _conv_module(h, w1, b1, w_dw, b_dw, ln_g, ln_b, w2, b2):
    z = h @ w1 + b1
    a, g = jnp.split(z, 2, axis=-1)
    z = a * jax.nn.sigmoid(g)
    zp = jnp.pad(z, ((0, 0), (CONV_WIDTH - 1, 0), (0, 0)))
    z = lax.conv_general_dilated(
        zp, w_dw[:, None, :], window_strides=(1,), padding='VALID',
        dimension_numbers=('NWC', 'WIO', 'NWC'), feature_group_count=D_CONV) + b_dw
    z = jax.nn.silu(_layernorm(z, ln_g, ln_b))
    return z @ w2 + b2

def _swiglu(h, wg, wu, wd):
    return (jax.nn.silu(h @ wg) * (h @ wu)) @ wd

def setup_inputs(seed: int = 0) -> dict:
    key = jax.random.key(seed)
    ks = jax.random.split(key, 24)
    f32 = jnp.float32
    nrm = lambda k, shape, scale: jax.random.normal(k, shape, f32) * scale
    return {
        "x": nrm(ks[0], (BATCH, SEQ, D_MODEL), 1.0),
        "w_in": nrm(ks[1], (N_EVEN, D_MODEL, IN_COLS), D_MODEL ** -0.5),
        "w_out": nrm(ks[2], (N_EVEN, D_MIX, D_MODEL), D_MIX ** -0.5),
        "a_ln_g": 1.0 + nrm(ks[3], (N_EVEN, D_A), 0.05),
        "a_ln_b": nrm(ks[4], (N_EVEN, D_A), 0.02),
        "a_ws": nrm(ks[5], (N_EVEN, N_HEADS_A, GMLP_BLOCK, GMLP_BLOCK), GMLP_BLOCK ** -0.5),
        "a_bs": 1.0 + nrm(ks[6], (N_EVEN, N_HEADS_A, GMLP_BLOCK), 0.1),
        "b_rel": nrm(ks[7], (N_EVEN, N_HEADS_B, N_REL), 0.2),
        "c_w1": nrm(ks[8], (N_ODD, D_MODEL, 2 * D_CONV), D_MODEL ** -0.5),
        "c_b1": nrm(ks[9], (N_ODD, 2 * D_CONV), 0.02),
        "c_dw": nrm(ks[10], (N_ODD, CONV_WIDTH, D_CONV), CONV_WIDTH ** -0.5),
        "c_bdw": nrm(ks[11], (N_ODD, D_CONV), 0.02),
        "c_ln_g": 1.0 + nrm(ks[12], (N_ODD, D_CONV), 0.05),
        "c_ln_b": nrm(ks[13], (N_ODD, D_CONV), 0.02),
        "c_w2": nrm(ks[14], (N_ODD, D_CONV, D_MODEL), D_CONV ** -0.5),
        "c_b2": nrm(ks[15], (N_ODD, D_MODEL), 0.02),
        "g_mix": 1.0 + nrm(ks[16], (DEPTH, D_MODEL), 0.05),
        "g_ffn": 1.0 + nrm(ks[17], (DEPTH, D_MODEL), 0.05),
        "f_wg": nrm(ks[18], (DEPTH, D_MODEL, D_FF), D_MODEL ** -0.5),
        "f_wu": nrm(ks[19], (DEPTH, D_MODEL, D_FF), D_MODEL ** -0.5),
        "f_wd": nrm(ks[20], (DEPTH, D_FF, D_MODEL), D_FF ** -0.5),
        "g_final": 1.0 + nrm(ks[21], (D_MODEL,), 0.05),
    }

def reference(x, w_in, w_out, a_ln_g, a_ln_b, a_ws, a_bs, b_rel,
              c_w1, c_b1, c_dw, c_bdw, c_ln_g, c_ln_b, c_w2, c_b2,
              g_mix, g_ffn, f_wg, f_wu, f_wd, g_final):
    split_pts = [D_A, 2 * D_A, 2 * D_A + D_B, 2 * D_A + 2 * D_B]
    for layer in range(DEPTH):
        i = layer // 2
        h = _rmsnorm(x, g_mix[layer])
        if layer % 2 == 0:
            proj = h @ w_in[i]
            u_a, v_a, q_b, k_b, v_b = jnp.split(proj, split_pts, axis=-1)
            y_a = _mixer_a(u_a, v_a, a_ln_g[i], a_ln_b[i], a_ws[i], a_bs[i])
            y_b = _mixer_b(q_b, k_b, v_b, b_rel[i])
            x = x + jnp.concatenate([y_a, y_b], axis=-1) @ w_out[i]
        else:
            x = x + _conv_module(h, c_w1[i], c_b1[i], c_dw[i], c_bdw[i],
                                 c_ln_g[i], c_ln_b[i], c_w2[i], c_b2[i])
        h = _rmsnorm(x, g_ffn[layer])
        x = x + _swiglu(h, f_wg[layer], f_wu[layer], f_wd[layer])
    return _rmsnorm(x, g_final)


_drawn_inputs = setup_inputs


def setup_inputs(seed=0):
    import zlib

    import numpy as np

    out = dict(_drawn_inputs(seed))
    spreads = {}
    factors = {'a_ln_g': 2.973,
     'a_ln_b': 7.28,
     'b_rel': 4.524,
     'c_b1': 5.29,
     'c_bdw': 3.173,
     'c_ln_b': 6.085,
     'c_b2': 3.855,
     'c_ln_g': 2.754}
    for name, (base, spread) in spreads.items():
        noise = np.random.default_rng([zlib.crc32(name.encode()), seed]).standard_normal(out[name].shape)
        drawn = base * np.exp(spread * noise) if base else spread * noise
        out[name] = __import__('jax').numpy.asarray(drawn.astype(out[name].dtype))
    for name, factor in factors.items():
        out[name] = (out[name] * factor).astype(out[name].dtype)
    return out
```

```python
from contextlib import ExitStack

import concourse.bass as bass
from concourse import mybir

F32 = mybir.dt.float32
F32R = mybir.dt.float32r
ALU = mybir.AluOpType
ACT = mybir.ActivationFunctionType
AX = mybir.AxisListType

P = 128
T = 1024
D = 1024
NT = D // P
HALF = 512
HEADS = 8
HD = 64
D_FF = 2816
FT = D_FF // P
GROUPS = (8, 8, 6)
CONV_W = 31
PAD = CONV_W - 1
EPS = 1e-6
NEG = -1e30
QUAD = 4
BAND = 640
SKEW = 256
EXT = 384
PROBS = 4

DMA_RING = 1024
SBUF_FREE = DMA_RING + 128
IN_CHUNKS = 20
COLS = {}
_at = 0
for _name, _n in (("g_mix", 16), ("g_ffn", 16), ("g_final", 8), ("c_b1", 16), ("c_bdw", 8), ("c_ln_g", 8),
                  ("c_ln_b", 8), ("c_b2", 8), ("c_dw", 8 * CONV_W)):
    COLS[_name] = _at
    _at += _n
N_COLS = _at


def build(nc, x, w_in, w_out, w_ws, b_bs, ln_g, ln_b, rel_ext, rel_far, per_channel, w_c1, w_c2, w_gu, w_dn, out):
    ctx = ExitStack()
    with ctx:
        K = 1024
        X0, PH, PL, RAW, WH, WL, RS, CON, ARENA = (SBUF_FREE + n for n in (
            0, 32 * K, 64 * K, 96 * K, 112 * K, 120 * K, 128 * K, 132 * K, 132 * K + 3328))
        QH, QL, TMP = ARENA, ARENA + 32 * K, ARENA + 64 * K

        def at(name, shape, offset, dt=F32):
            return nc.alloc_sbuf_tensor_at(name, shape, dt, offset=offset)

        xt = at("xt", [P, NT, T], X0)
        p_hi = at("p_hi", [P, NT, T], PH, F32R)
        p_lo = at("p_lo", [P, NT, T], PL, F32R)
        q_hi = at("q_hi", [P, NT, T], QH, F32R)
        q_lo = at("q_lo", [P, NT, T], QL, F32R)
        raw = at("raw", [P, QUAD, NT * P], RAW)
        w_hi = at("w_hi", [P, 2, NT * P], WH, F32R)
        w_lo = at("w_lo", [P, 2, NT * P], WL, F32R)
        rstd = at("rstd", [P, T], RS)
        chan = at("chan", [P, N_COLS], CON)
        ones = at("ones", [P, P], CON + 1536)
        ident = at("ident", [P, P], CON + 2048)
        small = at("small", [P, 64], CON + 2560)
        eps = small[:, 0:1]
        far = small[:, 1:9]
        assert N_COLS * 4 <= 1536
        au = at("au", [P, 8, T], QH)
        vb_tok = at("vb_tok", [P, 8, 512], QH)
        kb = at("kb", [P, 4, T], QL)
        qd = at("qd", [P, 4, T], QL + 16 * K)
        va_tok = at("va_tok", [P, 8, 512], QL + 16 * K)
        ws = at("ws", [P, HEADS, P], TMP)
        lng = at("lng", [P, 512], TMP + 4 * K)
        lnb = at("lnb", [P, 512], TMP + 6 * K)
        bsb = at("bsb", [P, 4, P], TMP + 8 * K)
        skew = at("skew", [P, HEADS, SKEW], TMP)
        q_fix = at("q_fix", [P, T], QH + 16 * K)
        v_fix = at("v_fix", [P, 8, P], QH + 20 * K)
        k_fix = at("k_fix", [P, T], QH + 24 * K)
        probs_t = at("probs_t", [P, BAND], QH + 28 * K)
        skew_fix = at("skew_fix", [P, 2, SKEW], TMP + 8 * K)
        probs = at("probs", [P, PROBS, BAND], TMP + 10 * K)
        sumsq = at("sumsq", [P, T], TMP + 10 * K)
        square = at("square", [P, T], TMP + 14 * K)
        gate = at("gate", [P, T], TMP)
        up = at("up", [P, T], TMP + 4 * K)
        act = at("act", [P, T], TMP + 18 * K)
        z_pad = at("z_pad", [P, T + PAD], PH)
        y_even = at("y_even", [P, NT, T], PL)
        y_odd = at("y_odd", [P, T], PH + 8 * K)
        mean_b = rstd
        o_fin = at("o_fin", [P, NT, T], PH)

        ps = nc.alloc_psum_tensor("ps", [P, 8, HALF], F32)

        def pair(j):
            return ps[:, 2 * j:2 * j + 2, :].rearrange("p a n -> p (a n)")

        rel_rows = nc.dram_tensor("rel_rows", (P, HEADS * EXT), F32, kind="Internal").ap()

        def sem(name):
            return nc.alloc_semaphore(name)

        x_loaded = [sem(f"x_loaded{n}") for n in range(NT)]
        chan_loaded, tables_loaded, rel_spread, skew_loaded = sem("chan_loaded"), sem("tables_loaded"), sem("rel_spread"), sem("skew_loaded")
        raw_loaded = [sem(f"raw_loaded{s}") for s in range(QUAD)]
        consts_set, ident_set, eps_set, ws_masked = sem("consts_set"), sem("ident_set"), sem("eps_set"), sem("ws_masked")
        w_hi_ready, w_lo_ready = sem("w_hi_ready"), sem("w_lo_ready")
        gemm_done, evacuated = sem("gemm_done"), sem("evacuated")
        h_hi_ready, h_ready = sem("h_hi_ready"), sem("h_ready")
        squared, sum_added = sem("squared"), sem("sum_added")
        stats_done, root_ready, rstd_ready = sem("stats_done"), sem("root_ready"), sem("rstd_ready")
        gelu_done = sem("gelu_done")
        va_turned, va_copied, vb_turned, vb_copied = sem("va_turned"), sem("va_copied"), sem("vb_turned"), sem("vb_copied")
        ln_stats, ln_var_ready, ln_root, va_step = sem("ln_stats"), sem("ln_var_ready"), sem("ln_root"), sem("va_step")
        gates_done, gates_evacuated, ya_ready = sem("gates_done"), sem("gates_evacuated"), sem("ya_ready")
        mix_hi_ready, mix_ready = sem("mix_hi_ready"), sem("mix_ready")
        fixed_ready, scores_done, near_biased, near_ready = sem("fixed_ready"), sem("scores_done"), sem("near_biased"), sem("near_ready")
        shift_ready, exp_done, prob_step, probs_ready = sem("shift_ready"), sem("exp_done"), sem("prob_step"), sem("probs_ready")
        probs_turned, probs_t_ready, pv_done = sem("probs_turned"), sem("probs_t_ready"), sem("pv_done")
        yb_hi_ready, skew_masked, mask_set = sem("yb_hi_ready"), sem("skew_masked"), sem("mask_set")
        silu_done, product_ready, act_hi_ready, act_ready = sem("silu_done"), sem("product_ready"), sem("act_hi_ready"), sem("act_ready")
        sigmoid_done, tap_done, conv_done, z_cleared = sem("sigmoid_done"), sem("tap_done"), sem("conv_done"), sem("z_cleared")
        cln_sums, cln_mean, cln_centred, cln_squared = sem("cln_sums"), sem("cln_mean"), sem("cln_centred"), sem("cln_squared")
        cln_root, cln_scaled, cln_silu, cln_step = sem("cln_root"), sem("cln_scaled"), sem("cln_silu"), sem("cln_step")
        conv_sum = sem("conv_sum")
        s_hi_ready, s_ready = sem("s_hi_ready"), sem("s_ready")
        out_ready, out_stored = sem("out_ready"), sem("out_stored")

        START = 1

        c_out = IN_CHUNKS
        at_chunk = c_out + 8
        ffn_at = []
        c_conv = c_proj = 0
        for layer in range(2):
            if layer == 1:
                c_conv, c_proj = at_chunk, at_chunk + 16
                at_chunk += 24
            groups, f0 = [], 0
            for g in GROUPS:
                groups.append((at_chunk, at_chunk + 2 * g, g, f0))
                at_chunk += 2 * g + 8
                f0 += g
            ffn_at.append(groups)
        chunks = at_chunk
        mask_q = small[0:1, 9:10]

        mask_row = at("mask_row", [1, P], CON + 2816)
        block = ctx.enter_context(nc.Block())

        @block.sync
        def _(sp):
            def load_quads(c0, quads, src):
                def quad(c, i):
                    for j in range(QUAD):
                        if type(c) is not int or c > 0:
                            sp.wait_ge(w_lo_ready, c + j - 3)
                        s = src(i, j)
                        sp.dma_start(raw[:, j, 0:s.shape[-1]], s).then_inc(raw_loaded[j], 16)
                if c0 == 0:
                    quad(0, 0)
                with sp.Fori(1 if c0 == 0 else 0, quads) as r:
                    i = sp.snap(r)
                    quad(i * QUAD + c0, i)

            sp.dma_start(chan[:, :], per_channel).then_inc(chan_loaded, 16)
            for n in range(NT):
                sp.dma_start(xt[:, n, :], x[n]).then_inc(x_loaded[n], 16)
                if n == 1:
                    for j in range(QUAD):
                        sp.dma_start(raw[:, j, :], w_in[j]).then_inc(raw_loaded[j], 16)
            sp.dma_start(ws[:, :, :], w_ws.rearrange("j h i -> j h i")).then_inc(tables_loaded, 16)
            sp.dma_start(lng[:, :], bass.AP(tensor=ln_g.tensor, offset=0, ap=[[0, P], [1, 512]])).then_inc(tables_loaded, 16)
            sp.dma_start(lnb[:, :], bass.AP(tensor=ln_b.tensor, offset=0, ap=[[0, P], [1, 512]])).then_inc(tables_loaded, 16)
            for hh in range(2):
                sp.dma_start(bsb[64 * hh:64 * hh + 64, :, :],
                             bass.AP(tensor=b_bs.tensor, offset=hh * P, ap=[[0, HD], [2 * P, 4], [1, P]])).then_inc(tables_loaded, 16)
            sp.dma_start(far, bass.AP(tensor=rel_far.tensor, offset=0, ap=[[0, P], [1, HEADS]])).then_inc(tables_loaded, 16)

            sp.dma_start(rel_rows, bass.AP(tensor=rel_ext.tensor, offset=0, ap=[[0, P], [1, HEADS * EXT]])).then_inc(rel_spread, 16)

            with sp.Fori(1, IN_CHUNKS // QUAD) as r:
                i = sp.snap(r)
                for j in range(QUAD):
                    sp.wait_ge(w_lo_ready, i * QUAD + (j - 3))
                    sp.dma_start(raw[:, j, :], w_in[i * QUAD + j]).then_inc(raw_loaded[j], 16)
            sp.wait_ge(rel_spread, 16)
            sp.wait_ge(gates_done, 4)
            sp.wait_ge(va_step, 24)
            sp.dma_start(skew[:, :, :], bass.AP(tensor=rel_rows.tensor, offset=P - 1, ap=[[HEADS * EXT - 1, P], [EXT, HEADS], [1, SKEW]])
                         ).then_inc(skew_loaded, 16)
            load_quads(c_out, 2, lambda i, j: w_out[i * QUAD + j])
            for layer in range(2):
                if layer == 1:
                    load_quads(c_conv, 4, lambda i, j: w_c1[i * QUAD + j])
                    load_quads(c_proj, 2, lambda i, j: w_c2[i * QUAD + j])
                for c_up, c_dn, g, f0 in ffn_at[layer]:
                    load_quads(c_up, 2 * g // QUAD, lambda i, j: w_gu[layer, i * QUAD + (2 * f0 + j)])
                    load_quads(c_dn, 2, lambda i, j: w_dn[layer, i * QUAD + j, :, f0 * P:(f0 + g) * P])
            for n in range(NT):
                sp.wait_ge(out_ready, n + 1)
                sp.dma_start(out[n], o_fin[:, n, :]).then_inc(out_stored, 16)
            sp.wait_ge(out_stored, 16 * NT)

        @block.gpsimd
        def _(pool):
            pool.memset(ones[:, :], 1.0).then_inc(consts_set, 1)
            pool.memset(eps, EPS).then_inc(eps_set, 1)
            pool.memset(ident[:, :], 0.0).then_inc(ident_set, 1)
            pool.wait_ge(ident_set, 1)
            pool.affine_select(out=ident[:, :], in_=ident[:, :], compare_op=ALU.not_equal, fill=1.0, base=0,
                               pattern=[[-1, P]], channel_multiplier=1).then_inc(ident_set, 1)
            pool.memset(mask_row[:, 0:64], 0.0).then_inc(mask_set, 1)
            pool.memset(mask_row[:, 64:P], NEG).then_inc(mask_set, 1)
            with pool.Fori(0, chunks // QUAD) as i:
                for j in range(QUAD):
                    pool.wait_ge(w_hi_ready, i * QUAD + (j + 1))
                    pool.tensor_tensor(w_lo[:, j % 2, :], raw[:, j, :], w_hi[:, j % 2, :].bitcast(F32), ALU.subtract
                                       ).then_inc(w_lo_ready, 1)

        @block.tensor
        def _(pe):
            def chunk(c, j, m_hi, m_lo, tiles, ready=None, free=None):
                pe.wait_ge(w_lo_ready, c + 1)
                if type(c) is not int or c >= QUAD:
                    pe.wait_ge(evacuated, c - 3)
                if free is not None:
                    pe.wait_ge(*free)
                for k in range(tiles):
                    if ready is not None:
                        pe.wait_ge(ready[0], ready[1](k))
                    hi, lo = (w[:, j % 2, k * P:(k + 1) * P] for w in (w_hi, w_lo))
                    for n, (w, m) in enumerate(((hi, m_hi), (hi, m_lo), (lo, m_hi))):
                        for half in range(2):
                            last = pe.matmul(ps[:, 2 * j + half, :], w, m[:, k, half * HALF:(half + 1) * HALF],
                                             start=(k == 0 and n == 0), stop=(k == tiles - 1 and n == 2))
                last.then_inc(gemm_done, 1)

            def quad(c, m_hi, m_lo, tiles, ready=None, free=None, stats=None):
                for j in range(QUAD):
                    if j == 3 and stats is not None:
                        pe.wait_ge(root_ready, stats + 1)
                    chunk(c + j, j, m_hi, m_lo, tiles, ready if j == 0 else None, free(j) if free else None)
                    if j == 0 and stats is not None:
                        norm_stats(stats)

            def quads(c0, n, m_hi, m_lo, tiles, ready, stats=None):
                first = 0
                if stats is not None:
                    quad(c0, m_hi, m_lo, tiles, ready, stats=stats)
                    first = 1
                with pe.Fori(first, n) as i:
                    quad(i * QUAD + c0, m_hi, m_lo, tiles, ready)

            def norm_stats(k):
                pe.wait_ge(sum_added, 9 * (k + 1))
                for half in range(2):
                    last = pe.matmul(ps[:, 6 + half, :], ones[:, :], sumsq[:, half * HALF:(half + 1) * HALF], start=True, stop=True)
                last.then_inc(stats_done, 1)

            def h_of(k):
                return (h_ready, lambda t: NT * k + t + 1)

            pe.sem_inc(pv_done, START)
            pe.sem_inc(probs_turned, PROBS)
            pe.wait_ge(consts_set, 1)
            quads(0, 2, p_hi, p_lo, NT, h_of(0), stats=0)
            pe.wait_ge(ident_set, 2)
            pe.wait_ge(gelu_done, 4)
            pe.wait_ge(evacuated, 8)
            for b in range(8):
                for m in range(4):
                    last = pe.transpose(ps[:, b, m * P:(m + 1) * P], au[:, m, b * P:(b + 1) * P], ident[:, :])
                last.then_inc(va_turned, 1)
            quad(8, p_hi, p_lo, NT, free=lambda j: (va_copied, 2 * j + 2))
            pe.wait_ge(va_step, 24)
            pe.wait_ge(ws_masked, 1)
            for m in range(4):
                pe.wait_ge(evacuated, 9 + m)
                for b in range(8):
                    for hh in range(2):
                        h = 2 * m + hh
                        last = pe.matmul(ps[64 * hh:64 * hh + 64, 2 * m + b // 4, (b % 4) * P:(b % 4 + 1) * P],
                                         va_tok[:, b, h * HD:(h + 1) * HD], ws[:, h, :], start=True, stop=True)
                last.then_inc(gates_done, 1)
            quad(12, p_hi, p_lo, NT, free=lambda j: (gates_evacuated, j + 1))
            pe.wait_ge(evacuated, 16)
            for b in range(8):
                for m in range(4):
                    last = pe.transpose(ps[:, b, m * P:(m + 1) * P], kb[:, m, b * P:(b + 1) * P], ident[:, :])
                last.then_inc(vb_turned, 1)
            quad(16, p_hi, p_lo, NT, free=lambda j: (vb_copied, 2 * j + 2))
            pe.wait_ge(evacuated, 20)
            pe.wait_ge(mask_set, 2)

            def scores(m, u):
                hh, t = u // 8, u % 8
                rows = slice(64 * hh, 64 * hh + 64)
                tiles = min(t + 1, 5)
                k0 = (t + 1 - tiles) * P
                near = min(tiles, 2) * P
                farther = tiles * P - near
                if u == 0:
                    pe.wait_ge(fixed_ready, m * 4 + 4)
                pe.wait_ge(exp_done, START + m * 16 + max(u - 1, 0))
                query = q_fix[rows, t * P:(t + 1) * P]
                if farther:
                    far_at = HALF - farther
                    pe.matmul(ps[:, 2 * (u % 2), far_at:HALF], query, k_fix[rows, k0:k0 + farther], start=True, stop=(t < 4))
                    if t >= 4:
                        pe.matmul(ps[:, 2 * (u % 2), far_at:far_at + 64], mask_row[:, :], ones[0:1, 0:64], start=False, stop=True)
                pe.matmul(ps[:, 2 * (u % 2) + 1, 0:near], query, k_fix[rows, k0 + farther:k0 + farther + near],
                          start=True, stop=True).then_inc(scores_done, 1)

            def turn(m, u):
                tiles = min(u % 8 + 1, 5)
                pe.wait_ge(probs_ready, m * 16 + (u + 1))
                pe.wait_ge(probs_t_ready, START + m * 16 + u)
                for k in range(tiles):
                    last = pe.transpose(ps[:, 4 + k // 4, (k % 4) * P:(k % 4 + 1) * P], probs[:, u % PROBS, k * P:(k + 1) * P], ident[:, :])
                last.then_inc(probs_turned, 1)

            def values(m, u):
                hh, t = u // 8, u % 8
                tiles = min(t + 1, 5)
                b0 = t + 1 - tiles
                pe.wait_ge(probs_t_ready, START + m * 16 + (u + 1))
                if u in (0, 4):
                    pe.wait_ge(mix_ready, m * 2 + 4)
                for k in range(tiles):
                    last = pe.matmul(ps[64 * hh:64 * hh + 64, 6 + t // 4, (t % 4) * P:(t % 4 + 1) * P],
                                     v_fix[:, b0 + k, 64 * hh:64 * hh + 64], probs_t[:, k * P:(k + 1) * P],
                                     start=(k == 0), stop=(k == tiles - 1))
                last.then_inc(pv_done, 1)

            with pe.Fori(0, 4) as m:
                for s in range(19):
                    if s < 16:
                        scores(m, s)
                    if 2 <= s < 18:
                        turn(m, s - 2)
                    if s >= 3:
                        values(m, s - 3)
            pe.wait_ge(mix_ready, 12)
            quads(c_out, 2, p_hi, p_lo, NT, (mix_ready, lambda k: 12))
            for layer in range(2):
                if layer == 1:
                    quads(c_conv, 4, q_hi, q_lo, NT, h_of(2), stats=2)
                    pe.wait_ge(evacuated, c_proj)
                    pe.wait_ge(conv_sum, NT + 1)
                    for half in range(2):
                        last = pe.matmul(ps[:, half, :], ones[:, :], sumsq[:, half * HALF:(half + 1) * HALF], start=True, stop=True)
                    last.then_inc(cln_sums, 1)
                    pe.wait_ge(cln_squared, NT + 1)
                    for half in range(2):
                        last = pe.matmul(ps[:, half, :], ones[:, :], sumsq[:, half * HALF:(half + 1) * HALF], start=True, stop=True)
                    last.then_inc(cln_sums, 1)
                    pe.wait_ge(cln_root, 1)
                    quads(c_proj, 2, p_hi, p_lo, NT, (s_ready, lambda k: k + 1))
                done = FT * layer
                for n, (c_up, c_dn, g, f0) in enumerate(ffn_at[layer]):
                    norm = 1 + 2 * layer
                    quads(c_up, 2 * g // QUAD, q_hi, q_lo, NT, h_of(norm), stats=norm if n == 0 else None)
                    base = done + f0
                    quads(c_dn, 2, p_hi, p_lo, g, (act_ready, lambda k: START + base + k + 1))
            norm_stats(4)

        @block.scalar
        def _(se):
            def apart():
                se.wait_ge(eps_set, 1)

            def split_ahead(c, j):
                s = (j + 2) % QUAD
                if type(c) is int and c + 2 >= chunks:
                    return
                q = c + (2 - s)
                se.wait_ge(raw_loaded[s], q * 4 + 16)
                if type(c) is not int or c >= 0:
                    se.wait_ge(gemm_done, c + 1)
                se.activation(w_hi[:, s % 2, :], raw[:, s, :], ACT.Copy).then_inc(w_hi_ready, 1)

            def quads(c0, n, work=None, tail=False):
                def body(i, c):
                    for j in range(QUAD):
                        split_ahead(c + j, j)
                        if work is not None:
                            work(i, j, c + j)
                with se.Fori(0, n - 1 if tail else n) as i:
                    body(i, i * QUAD + c0)
                if tail:
                    body(n - 1, (n - 1) * QUAD + c0)

            def prepare(k, n, gain, hi, split=True):
                se.wait_ge(sum_added, n + (9 * k + 1))
                if type(n) is not int:
                    apart()
                if split:
                    se.activation(hi[:, n, :], xt[:, n, :], ACT.Copy, scale=gain).then_inc(h_hi_ready, 1)
                se.activation(square[:, :], xt[:, n, :], ACT.Square).then_inc(squared, 1)

            def root(k):
                se.wait_ge(stats_done, k + 1)
                se.activation(rstd[:, :], pair(3), ACT.Sqrt, bias=eps, scale=1.0 / D).then_inc(root_ready, 1)

            def gain(name, n):
                return chan[:, bass.ds(n + COLS[name], 1)]

            se.sem_inc(exp_done, START)
            se.sem_inc(probs_t_ready, START)
            se.wait_ge(chan_loaded, 16)
            for n in range(NT):
                se.wait_ge(x_loaded[n], 16)
                prepare(0, n, gain("g_mix", n), p_hi)
                if n == 1:
                    split_ahead(-2, 2)
                    split_ahead(-1, 3)
            se.wait_ge(eps_set, 1)
            root(0)

            def gelu(i, j, c):
                se.wait_ge(evacuated, c + 1)
                tile = au[:, i * QUAD + j, :]
                apart()
                se.activation(tile, tile, ACT.Gelu_apprx_tanh).then_inc(gelu_done, 1)

            quads(0, 2, gelu)
            for b in range(8):
                se.wait_ge(va_turned, b + 1)
                se.activation(va_tok[:, b, :], ps[:, b, :], ACT.Copy).then_inc(va_copied, 1)
            se.wait_ge(ln_stats, 16)
            se.activation(small[:, 32:40], small[:, 16:32].rearrange("p (b s) -> p b s", s=2)[:, :, 1], ACT.Sqrt, bias=eps
                          ).then_inc(ln_root, 1)
            quads(8, 2)
            for b in range(8):
                se.wait_ge(vb_turned, b + 1)
                se.activation(vb_tok[:, b, :], ps[:, b, :], ACT.Copy).then_inc(vb_copied, 1)
            quads(16, 1)
            for m in range(4):
                se.wait_ge(gemm_done, IN_CHUNKS)
                se.wait_ge(ya_ready, m + 1)
                se.activation(p_hi[:, m, :], au[:, 4 + m, :], ACT.Copy).then_inc(mix_hi_ready, 1)

            def exps(m, u):
                tiles = min(u % 8 + 1, 5)
                near = min(tiles, 2) * P
                farther = tiles * P - near
                s = 40 + 8 * (u % 2)
                se.wait_ge(probs_turned, m * 16 + (u + 1))
                se.wait_ge(shift_ready, m * 16 + (u + 1))
                se.activation(probs[:, u % PROBS, 0:tiles * P], pair(u % 2)[:, HALF - farther:HALF + near], ACT.Exp,
                              bias=small[:, s + 2:s + 3], accum_out=small[:, s + 3:s + 4]).then_inc(exp_done, 1)

            def copy_turned(m, u):
                n = min(u % 8 + 1, 5) * P
                se.wait_ge(probs_turned, m * 16 + (u + 1 + PROBS))
                se.wait_ge(pv_done, START + m * 16 + u)
                se.activation(probs_t[:, 0:n], pair(2)[:, 0:n], ACT.Copy).then_inc(probs_t_ready, 1)

            def output(m, half):
                se.wait_ge(pv_done, START + m * 16 + (12 + 4 * half))
                apart()
                se.activation(p_hi[:, m + 4, half * HALF:(half + 1) * HALF], ps[:, 6 + half, :], ACT.Copy).then_inc(yb_hi_ready, 1)

            with se.Fori(0, 4) as m:
                for s in range(18):
                    if s < 16:
                        exps(m, s)
                    if s >= 2:
                        copy_turned(m, s - 2)
                    if s == 16:
                        output(m, 0)
                output(m, 1)

            def down(k, name, hi):
                def work(i, j, c):
                    se.wait_ge(evacuated, c + 1)
                    n = i * QUAD + j
                    prepare(k, n, gain(name, n + (8 if name == "g_mix" or k == 3 else 0)), hi, split=k < 4)
                return work

            quads(c_out, 2, down(1, "g_ffn", q_hi))
            for layer in range(2):
                if layer == 1:
                    root(2)

                    def sigmoid(i, j, c):
                        if j % 2:
                            n = i * 2 + j // 2
                            se.wait_ge(evacuated, c + 1)
                            apart()
                            se.activation(act[:, :], up[:, :], ACT.Sigmoid, bias=gain("c_b1", n + 8)).then_inc(sigmoid_done, 1)
                    quads(c_conv, 4, sigmoid)
                    se.wait_ge(cln_sums, 1)
                    se.activation(mean_b[:, :], pair(0), ACT.Copy, scale=1.0 / D).then_inc(cln_mean, 1)
                    for n in range(NT):
                        se.wait_ge(cln_centred, n + 1)
                        se.wait_ge(cln_squared, n + 1)
                        se.activation(square[:, :], y_even[:, n, :], ACT.Square).then_inc(cln_step, 1)
                    se.wait_ge(cln_sums, 2)
                    se.activation(mean_b[:, :], pair(0), ACT.Sqrt, bias=eps, scale=1.0 / D).then_inc(cln_root, 1)
                    for n in range(NT):
                        se.wait_ge(cln_scaled, n + 2)
                        buf = (gate, up)[n % 2]
                        se.activation(buf[:, :], buf[:, :], ACT.Silu, scale=gain("c_ln_g", n), bias=gain("c_ln_b", n)).then_inc(cln_silu, 1)
                        se.wait_ge(cln_silu, n + 1)
                        se.activation(p_hi[:, n, :], buf[:, :], ACT.Copy).then_inc(s_hi_ready, 1)
                    quads(c_proj, 2, down(3, "g_ffn", q_hi))
                norm = 1 + 2 * layer
                root(norm)
                for n, (c_up, c_dn, g, f0) in enumerate(ffn_at[layer]):
                    base = FT * layer + f0

                    def inner(i, j, c):
                        f = i * 2 + (base + j // 2)
                        if j % 2 == 0:
                            se.wait_ge(evacuated, c + 1)
                            se.wait_ge(product_ready, START + f)
                            se.activation(act[:, :], gate[:, :], ACT.Silu).then_inc(silu_done, 1)
                        else:
                            se.wait_ge(product_ready, START + f + 1)
                            apart()
                            se.activation(p_hi[:, i * 2 + j // 2, :], up[:, :], ACT.Copy).then_inc(act_hi_ready, 1)
                    quads(c_up, 2 * g // QUAD, inner)
                    last = n == len(GROUPS) - 1
                    work = down(2 + 2 * layer, "g_mix", q_hi) if last else None
                    quads(c_dn, 2, work, tail=last and layer == 1)
            root(4)

        @block.vector
        def _(ve):
            def evacuate(c, j, dst, factor=None):
                ve.wait_ge(gemm_done, c + 1)
                if factor is None:
                    ve.tensor_tensor(dst, pair(j), rstd[:, :], ALU.mult).then_inc(evacuated, 1)
                else:
                    ve.scalar_tensor_tensor(out=dst, in0=pair(j), scalar=factor, in1=rstd[:, :], op0=ALU.mult, op1=ALU.mult
                                            ).then_inc(evacuated, 1)

            def quads(c0, n, work):
                with ve.Fori(0, n) as i:
                    for j in range(QUAD):
                        work(i, j, i * QUAD + (c0 + j))

            def clear_sum(k):
                if k:
                    ve.wait_ge(stats_done, k)
                ve.memset(sumsq[:, :], 0.0).then_inc(sum_added, 1)

            def prepare(k, n, gain, hi, lo, split=True):
                if split:
                    ve.wait_ge(h_hi_ready, n + (NT * k + 1))
                    ve.scalar_tensor_tensor(out=lo[:, n, :], in0=xt[:, n, :], scalar=gain, in1=hi[:, n, :].bitcast(F32),
                                            op0=ALU.mult, op1=ALU.subtract).then_inc(h_ready, 1)
                ve.wait_ge(squared, n + (NT * k + 1))
                ve.wait_ge(sum_added, n + (9 * k + 1))
                ve.tensor_tensor(sumsq[:, :], sumsq[:, :], square[:, :], ALU.add).then_inc(sum_added, 1)

            def invert(k):
                ve.wait_ge(root_ready, k + 1)
                ve.reciprocal(rstd[:, :], rstd[:, :]).then_inc(rstd_ready, 1)
                ve.wait_ge(rstd_ready, k + 1)

            def gain(name, n):
                return chan[:, bass.ds(n + COLS[name], 1)]

            for counted in (product_ready, act_ready, tap_done):
                ve.sem_inc(counted, START)
            clear_sum(0)
            ve.wait_ge(chan_loaded, 16)
            for n in range(NT):
                ve.wait_ge(x_loaded[n], 16)
                prepare(0, n, gain("g_mix", n), p_hi, p_lo)
            ve.wait_ge(tables_loaded, 16 * 6)
            ve.memset(ws[64:P, :, 0:64], 0.0).then_inc(ws_masked, 1)
            invert(0)
            quads(0, 2, lambda i, j, c: evacuate(c, j, au[:, i * QUAD + j, :]))
            for b in range(8):
                ve.wait_ge(va_copied, b + 1)
                ve.bn_stats(square[:, 6 * b:6 * b + 6], va_tok[:, b, :]).then_inc(ln_stats, 1)
            ve.wait_ge(ln_stats, 8)
            for b in range(8):
                ve.bn_aggr(small[:, 16 + 2 * b:18 + 2 * b], square[:, 6 * b:6 * b + 6]).then_inc(ln_stats, 1)
            ve.wait_ge(ln_root, 1)
            ve.reciprocal(small[:, 32:40], small[:, 32:40]).then_inc(ln_var_ready, 1)
            ve.wait_ge(ln_var_ready, 1)
            ve.wait_ge(ln_stats, 16)
            for b in range(8):
                ve.tensor_scalar(va_tok[:, b, :], va_tok[:, b, :], small[:, 16 + 2 * b:17 + 2 * b], small[:, 32 + b:33 + b],
                                 ALU.subtract, ALU.mult).then_inc(va_step, 1)
            ve.wait_ge(va_step, 8)
            for b in range(8):
                ve.tensor_tensor(va_tok[:, b, :], va_tok[:, b, :], lng[:, :], ALU.mult).then_inc(va_step, 1)
            ve.wait_ge(va_step, 16)
            for b in range(8):
                ve.tensor_tensor(va_tok[:, b, :], va_tok[:, b, :], lnb[:, :], ALU.add).then_inc(va_step, 1)
            for j in range(QUAD):
                evacuate(8 + j, j, kb[:, j, :])
            for m in range(4):
                buf = (square, sumsq)[m % 2]
                ve.wait_ge(gates_done, m + 1)
                ve.tensor_tensor(buf[:, :].rearrange("p (b i) -> p b i", i=P), pair(m).rearrange("p (b i) -> p b i", i=P),
                                 bass.AP(tensor=bsb[:, m, :].tensor, offset=bsb[:, m, :].offset,
                                         ap=[list(bsb[:, m, :].ap[0]), [0, 8], [1, P]]), ALU.add).then_inc(gates_evacuated, 1)
                ve.wait_ge(gates_evacuated, m + 1)
                ve.wait_ge(gelu_done, 8)
                ve.tensor_tensor(au[:, 4 + m, :], buf[:, :], au[:, 4 + m, :], ALU.mult).then_inc(ya_ready, 1)
            for j in range(QUAD):
                evacuate(12 + j, j, qd[:, j, :], float(HD) ** -0.5)
            for j in range(QUAD):
                evacuate(16 + j, j, kb[:, j, :])
            for m in range(4):
                ve.wait_ge(mix_hi_ready, m + 1)
                ve.tensor_tensor(p_lo[:, m, :], au[:, 4 + m, :], p_hi[:, m, :].bitcast(F32), ALU.subtract).then_inc(mix_ready, 1)
            ve.wait_ge(skew_loaded, 16)
            ve.memset(skew[0:64, :, SKEW - 64:SKEW], NEG).then_inc(skew_masked, 1)
            ve.wait_ge(skew_masked, 1)
            ve.tensor_tensor(skew[:, :, :], skew[:, :, :], bass.AP(tensor=far.tensor, offset=far.offset,
                             ap=[list(far.ap[0]), [1, HEADS], [0, SKEW]]), ALU.subtract).then_inc(skew_masked, 1)
            ve.wait_ge(skew_masked, 2)
            ve.wait_ge(evacuated, IN_CHUNKS)
            ve.wait_ge(mix_ready, 4)

            def maxima(m, u):
                hh, t = u // 8, u % 8
                tiles = min(t + 1, 5)
                near = min(tiles, 2) * P
                farther = tiles * P - near
                s = 40 + 8 * (u % 2)
                ve.wait_ge(scores_done, m * 16 + (u + 1))
                scored = ps[:, 2 * (u % 2) + 1, 0:near]
                biases = skew_fix[:, hh, SKEW - near:SKEW]
                if farther:
                    ve.tensor_reduce(small[:, s:s + 1], ps[:, 2 * (u % 2), HALF - farther:HALF], AX.X, ALU.max)
                    ve.tensor_tensor_reduce(scored, scored, biases, 1.0, NEG, ALU.add, ALU.max, small[:, s + 1:s + 2]
                                            ).then_inc(near_ready, 1)
                else:
                    ve.tensor_tensor(scored, scored, biases, ALU.add).then_inc(near_biased, 1)
                    ve.wait_ge(near_biased, m * 4 + ((u % 8) + 1 + 2 * hh))
                    ve.tensor_reduce(small[:, s + 1:s + 2], scored, AX.X, ALU.max).then_inc(near_ready, 1)

            def shift(m, u):
                s = 40 + 8 * (u % 2)
                ve.wait_ge(near_ready, m * 16 + (u + 1))
                if u % 8 >= 2:
                    ve.tensor_scalar(small[:, s + 2:s + 3], small[:, s:s + 1], small[:, s + 1:s + 2], -1.0, ALU.max, ALU.mult
                                     ).then_inc(shift_ready, 1)
                else:
                    ve.tensor_scalar(small[:, s + 2:s + 3], small[:, s + 1:s + 2], -1.0, None, ALU.mult).then_inc(shift_ready, 1)

            def invert_sum(m, u):
                s = 40 + 8 * (u % 2)
                ve.wait_ge(exp_done, START + m * 16 + (u + 1))
                ve.reciprocal(small[:, s + 4:s + 5], small[:, s + 3:s + 4]).then_inc(prob_step, 1)

            def normalise(m, u):
                s = 40 + 8 * (u % 2)
                n = min(u % 8 + 1, 5) * P
                ve.wait_ge(prob_step, m * 16 + (u + 1))
                ve.tensor_scalar(probs[:, u % PROBS, 0:n], probs[:, u % PROBS, 0:n], small[:, s + 4:s + 5], None, ALU.mult
                                 ).then_inc(probs_ready, 1)

            def output(m, half):
                ve.wait_ge(yb_hi_ready, m * 2 + (half + 1))
                cols = slice(half * HALF, (half + 1) * HALF)
                ve.tensor_tensor(p_lo[:, m + 4, cols], ps[:, 6 + half, :], p_hi[:, m + 4, cols].bitcast(F32), ALU.subtract
                                 ).then_inc(mix_ready, 1)

            with ve.Fori(0, 4) as m:
                ve.wait_ge(pv_done, START + m * 16)
                ve.tensor_copy(q_fix[:, :], qd[:, m, :]).then_inc(fixed_ready, 1)
                ve.tensor_copy(k_fix[:, :], kb[:, m, :]).then_inc(fixed_ready, 1)
                ve.tensor_copy(v_fix[:, :, :], vb_tok[:, :, bass.ds(m * P, P)]).then_inc(fixed_ready, 1)
                ve.tensor_copy(skew_fix[:, :, :], skew[:, bass.ds(m * 2, 2), :]).then_inc(fixed_ready, 1)
                ve.wait_ge(fixed_ready, m * 4 + 4)
                for s in range(17):
                    if s < 16:
                        maxima(m, s)
                    if s >= 1:
                        invert_sum(m, s - 1)
                    if s < 16:
                        shift(m, s)
                    if s >= 1:
                        normalise(m, s - 1)
                output(m, 0)
                output(m, 1)

            def down(k, name, bias=None):
                def work(i, j, c):
                    n = i * QUAD + j
                    ve.wait_ge(gemm_done, c + 1)
                    if bias is None:
                        ve.tensor_tensor(xt[:, n, :], pair(j), xt[:, n, :], ALU.add).then_inc(evacuated, 1)
                    else:
                        ve.scalar_tensor_tensor(out=xt[:, n, :], in0=pair(j), scalar=gain(bias, n), in1=xt[:, n, :],
                                                op0=ALU.add, op1=ALU.add).then_inc(evacuated, 1)
                    if k is not None:
                        ve.wait_ge(evacuated, c + 1)
                        prepare(k, n, gain(name, n + (8 if name == "g_mix" or k == 3 else 0)), q_hi, q_lo, split=k < 4)
                return work

            clear_sum(1)
            quads(c_out, 2, down(1, "g_ffn"))
            for layer in range(2):
                if layer == 1:
                    invert(2)
                    ve.memset(z_pad[:, 0:PAD], 0.0).then_inc(z_cleared, 1)
                    ve.wait_ge(z_cleared, 1)
                    ve.wait_ge(stats_done, 3)
                    ve.memset(sumsq[:, :], 0.0).then_inc(conv_sum, 1)
                    TAPS = CONV_W + 2

                    def conv(i, j, c):
                        n = i * 2 + j // 2
                        if j % 2 == 0:
                            ve.wait_ge(tap_done, START + n * TAPS)
                            evacuate(c, j, gate[:, :])
                            return
                        evacuate(c, j, up[:, :])
                        ve.wait_ge(sigmoid_done, n + 1)
                        ve.scalar_tensor_tensor(out=z_pad[:, PAD:PAD + T], in0=gate[:, :], scalar=gain("c_b1", n), in1=act[:, :],
                                                op0=ALU.add, op1=ALU.mult).then_inc(tap_done, 1)
                        ve.wait_ge(tap_done, START + n * TAPS + 1)

                        def tap(k):
                            return chan[:, bass.ds(n * CONV_W + (COLS["c_dw"] + k), 1)]
                        ve.tensor_scalar(y_even[:, n, :], z_pad[:, 0:T], tap(0), gain("c_bdw", n), ALU.mult, ALU.add).then_inc(tap_done, 1)
                        ve.tensor_scalar(y_odd[:, :], z_pad[:, 1:1 + T], tap(1), None, ALU.mult).then_inc(tap_done, 1)
                        for k in range(2, CONV_W):
                            y = y_odd[:, :] if k % 2 else y_even[:, n, :]
                            ve.wait_ge(tap_done, START + n * TAPS + k)
                            ve.scalar_tensor_tensor(out=y, in0=z_pad[:, k:k + T], scalar=tap(k), in1=y, op0=ALU.mult, op1=ALU.add
                                                    ).then_inc(tap_done, 1)
                        ve.wait_ge(tap_done, START + n * TAPS + (CONV_W + 1))
                        ve.tensor_tensor(y_even[:, n, :], y_even[:, n, :], y_odd[:, :], ALU.add).then_inc(tap_done, 1)
                        ve.wait_ge(tap_done, START + n * TAPS + (CONV_W + 2))
                        ve.wait_ge(conv_sum, n + 1)
                        ve.tensor_tensor(sumsq[:, :], sumsq[:, :], y_even[:, n, :], ALU.add).then_inc(conv_sum, 1)
                    quads(c_conv, 4, conv)
                    ve.wait_ge(cln_mean, 1)
                    ve.memset(sumsq[:, :], 0.0).then_inc(cln_squared, 1)
                    for n in range(NT):
                        ve.tensor_tensor(y_even[:, n, :], y_even[:, n, :], mean_b[:, :], ALU.subtract).then_inc(cln_centred, 1)
                    for n in range(NT):
                        ve.wait_ge(cln_step, n + 1)
                        ve.wait_ge(cln_squared, n + 1)
                        ve.tensor_tensor(sumsq[:, :], sumsq[:, :], square[:, :], ALU.add).then_inc(cln_squared, 1)
                    ve.wait_ge(cln_root, 1)
                    ve.reciprocal(mean_b[:, :], mean_b[:, :]).then_inc(cln_scaled, 1)
                    ve.wait_ge(cln_scaled, 1)

                    def conv_low(n):
                        ve.wait_ge(s_hi_ready, n + 1)
                        buf = (gate, up)[n % 2]
                        ve.tensor_tensor(p_lo[:, n, :], buf[:, :], p_hi[:, n, :].bitcast(F32), ALU.subtract).then_inc(s_ready, 1)

                    for n in range(NT):
                        if n >= 2:
                            conv_low(n - 2)
                            ve.wait_ge(s_ready, n - 1)
                        buf = (gate, up)[n % 2]
                        ve.tensor_tensor(buf[:, :], y_even[:, n, :], mean_b[:, :], ALU.mult).then_inc(cln_scaled, 1)
                    conv_low(NT - 2)
                    conv_low(NT - 1)
                    ve.wait_ge(cln_sums, 2)
                    clear_sum(3)
                    quads(c_proj, 2, down(3, "g_ffn", bias="c_b2"))
                norm = 1 + 2 * layer
                invert(norm)
                clear_sum(2 + 2 * layer)
                for n, (c_up, c_dn, g, f0) in enumerate(ffn_at[layer]):
                    base = FT * layer + f0

                    def inner(i, j, c):
                        f = i * 2 + (base + j // 2)
                        if j % 2 == 0:
                            evacuate(c, j, gate[:, :])
                            return
                        ve.wait_ge(act_ready, START + f)
                        evacuate(c, j, up[:, :])
                        ve.wait_ge(silu_done, f + 1)
                        ve.wait_ge(evacuated, c + 1)
                        ve.tensor_tensor(up[:, :], up[:, :], act[:, :], ALU.mult).then_inc(product_ready, 1)
                        ve.wait_ge(act_hi_ready, f + 1)
                        k = i * 2 + j // 2
                        ve.tensor_tensor(p_lo[:, k, :], up[:, :], p_hi[:, k, :].bitcast(F32), ALU.subtract).then_inc(act_ready, 1)
                    quads(c_up, 2 * g // QUAD, inner)
                    last = n == len(GROUPS) - 1
                    quads(c_dn, 2, down(2 + 2 * layer if last else None, "g_mix"))
            invert(4)
            for n in range(NT):
                ve.scalar_tensor_tensor(out=o_fin[:, n, :], in0=xt[:, n, :], scalar=gain("g_final", n), in1=rstd[:, :],
                                        op0=ALU.mult, op1=ALU.mult).then_inc(out_ready, 1)


def kernel(x, w_in, w_out, a_ln_g, a_ln_b, a_ws, a_bs, b_rel, c_w1, c_b1, c_dw, c_bdw, c_ln_g, c_ln_b, c_w2, c_b2,
           g_mix, g_ffn, f_wg, f_wu, f_wd, g_final):
    import numpy as np
    import concourse.bacc as bacc
    from concourse import mybir as mb
    from concourse.bass_utils import run_bass_kernel_spmd

    def by_chunk(w):
        w = np.asarray(w)
        k, n = w.shape
        return w.reshape(k // P, P, n // P, P).transpose(2, 1, 0, 3).reshape(n // P, P, k)

    def by_partition(v):
        v = np.asarray(v)
        return v.reshape(-1, P).T

    wi = by_chunk(w_in[0])
    order = [4, 5, 6, 7, 0, 1, 2, 3, 16, 17, 18, 19, 8, 9, 10, 11, 12, 13, 14, 15]
    c1 = by_chunk(c_w1[0])
    rel = np.asarray(b_rel)[0][:, ::-1]
    ext = np.concatenate([np.broadcast_to(rel[:, :1], (HEADS, P - 1)), rel[:, :EXT - P + 1]], axis=1)
    dw = np.asarray(c_dw)[0].T.reshape(NT, P, CONV_W).transpose(1, 0, 2).reshape(P, NT * CONV_W)
    arrays = {
        "x": np.asarray(x)[0].T.reshape(NT, P, T),
        "w_in": wi[order],
        "w_out": by_chunk(w_out[0]),
        "w_ws": np.asarray(a_ws)[0].transpose(2, 0, 1),
        "b_bs": np.asarray(a_bs)[0],
        "ln_g": np.asarray(a_ln_g),
        "ln_b": np.asarray(a_ln_b),
        "rel_ext": ext,
        "rel_far": rel[:, :1].reshape(1, HEADS),
        "per_channel": np.concatenate([by_partition(v) for v in (g_mix, g_ffn, g_final, c_b1, c_bdw, c_ln_g, c_ln_b, c_b2)] + [dw], axis=1),
        "w_c1": np.stack([c1[:NT], c1[NT:]], axis=1).reshape(2 * NT, P, D),
        "w_c2": by_chunk(c_w2[0]),
        "w_gu": np.stack([np.stack([by_chunk(f_wg[n]), by_chunk(f_wu[n])], axis=1).reshape(2 * FT, P, D) for n in range(2)]),
        "w_dn": np.stack([by_chunk(f_wd[n]) for n in range(2)]),
    }
    arrays = {k: np.ascontiguousarray(v) for k, v in arrays.items()}
    nc = bacc.Bacc("TRN2", target_bir_lowering=False, num_devices=1, dynamic_dma_scratch_size=DMA_RING)
    args = {k: nc.dram_tensor(f"in_{k}", v.shape, mb.dt.from_np(v.dtype), kind="ExternalInput").ap() for k, v in arrays.items()}
    args["out"] = nc.dram_tensor("out", (NT, P, T), mb.dt.float32, kind="ExternalOutput").ap()
    build(nc, **args)
    r = run_bass_kernel_spmd(nc, [{f"in_{k}": v for k, v in arrays.items()}], core_ids=[0])
    return np.ascontiguousarray(r.results[0]["out"].reshape(D, T).T).reshape(1, T, D)
```

```python
from contextlib import ExitStack

import concourse.bass as bass
from concourse import mybir

F32 = mybir.dt.float32
F32R = mybir.dt.float32r
ALU = mybir.AluOpType
ACT = mybir.ActivationFunctionType
AX = mybir.AxisListType

P = 128
T = 1024
D = 1024
NT = D // P
HALF = 512
HEADS = 8
HD = 64
D_FF = 2816
FT = D_FF // P
GROUPS = (8, 8, 6)
CONV_W = 31
PAD = CONV_W - 1
EPS = 1e-6
NEG = -1e30
QUAD = 4
PAIR = 2
BAND = 640
SKEW = 256
EXT = 384
PROBS = 4
UNITS = 16
AHEAD = 4
FILL = (4, 4, 4, 4, 4, 4, 3, 3, 2) + (0,) * 7
HALF_ENDS = (1, 3, 5, 8)

DMA_RING = 1024
SBUF_FREE = DMA_RING + 128
IN_CHUNKS = 20
PRE_CHUNKS = 14
COLS = {}
_at = 0
for _name, _n in (("g_mix", 16), ("g_ffn", 16), ("g_final", 8), ("c_b1", 16), ("c_bdw", 8), ("c_ln_g", 8),
                  ("c_ln_b", 8), ("c_b2", 8), ("c_dw", 8 * CONV_W)):
    COLS[_name] = _at
    _at += _n
N_COLS = _at


def build(nc, x, w_in, w_out, w_ws, b_bs, ln_g, ln_b, rel_ext, rel_far, per_channel, w_c1, w_c2, w_gu, w_dn, out):
    ctx = ExitStack()
    with ctx:
        K = 1024
        X0, PH, PL, RAW, WH, WL, RS, CON, ARENA = (SBUF_FREE + n for n in (
            0, 32 * K, 64 * K, 96 * K, 112 * K, 120 * K, 128 * K, 132 * K, 132 * K + 3328))
        QH, QL, TMP = ARENA, ARENA + 32 * K, ARENA + 64 * K

        def at(name, shape, offset, dt=F32):
            return nc.alloc_sbuf_tensor_at(name, shape, dt, offset=offset)

        xt = at("xt", [P, NT, T], X0)
        p_hi = at("p_hi", [P, NT, T], PH, F32R)
        p_lo = at("p_lo", [P, NT, T], PL, F32R)
        q_hi = at("q_hi", [P, NT, T], QH, F32R)
        q_lo = at("q_lo", [P, NT, T], QL, F32R)
        raw = at("raw", [P, PAIR, NT * P], RAW)
        w_hi = at("w_hi", [P, 2, NT * P], WH, F32R)
        w_lo = at("w_lo", [P, 2, NT * P], WL, F32R)
        rstd = at("rstd", [P, T], RS)
        chan = at("chan", [P, N_COLS], CON)
        ones = at("ones", [P, P], CON + 1536)
        ident = at("ident", [P, P], CON + 2048)
        small = at("small", [P, 64], CON + 2560)
        eps = small[:, 0:1]
        far = small[:, 1:9]
        assert N_COLS * 4 <= 1536
        au = at("au", [P, 8, T], QH)
        vb_tok = at("vb_tok", [P, 8, 512], QH)
        vb = at("vb", [P, 4, T], QL)
        va_tok = at("va_tok", [P, 8, 512], QL + 16 * K)
        ws = at("ws", [P, HEADS, P], TMP)
        lng = at("lng", [P, 512], TMP + 4 * K)
        lnb = at("lnb", [P, 512], TMP + 6 * K)
        bsb = at("bsb", [P, 4, P], TMP + 8 * K)
        skew = at("skew", [P, HEADS, SKEW], TMP)
        q_fix = at("q_fix", [P, T], QL + 16 * K)
        k_fix = at("k_fix", [P, T], QL + 20 * K)
        v_fix = at("v_fix", [P, 8, P], QL + 24 * K)
        q_next = at("q_next", [P, T], QL + 28 * K)
        k_next = at("k_next", [P, T], QL + 12 * K)
        yb = at("yb", [P, 3, T], QL)
        probs_t = at("probs_t", [P, BAND], TMP + 20 * K)
        skew_fix = at("skew_fix", [P, 2, SKEW], TMP + 8 * K)
        probs = at("probs", [P, PROBS, BAND], TMP + 10 * K)
        sumsq = at("sumsq", [P, T], TMP + 10 * K)
        square = at("square", [P, T], TMP + 14 * K)
        gate = at("gate", [P, T], TMP)
        up = at("up", [P, T], TMP + 4 * K)
        act = at("act", [P, T], TMP + 18 * K)
        z_pad = at("z_pad", [P, T + PAD], PH)
        y_even = at("y_even", [P, NT, T], PL)
        y_odd = at("y_odd", [P, T], PH + 8 * K)
        mean_b = rstd
        o_fin = at("o_fin", [P, NT, T], PH)

        ps = nc.alloc_psum_tensor("ps", [P, 8, HALF], F32)

        def pair(j):
            return ps[:, 2 * j:2 * j + 2, :].rearrange("p a n -> p (a n)")


        rel_rows = nc.dram_tensor("rel_rows", (P, HEADS * EXT), F32, kind="Internal").ap()

        def sem(name):
            return nc.alloc_semaphore(name)

        x_loaded = [sem(f"x_loaded{n}") for n in range(NT)]
        chan_loaded, tables_loaded, rel_spread, skew_loaded = sem("chan_loaded"), sem("tables_loaded"), sem("rel_spread"), sem("skew_loaded")
        raw_loaded = [sem(f"raw_loaded{s}") for s in range(PAIR)]
        consts_set, ident_set, eps_set, ws_masked = sem("consts_set"), sem("ident_set"), sem("eps_set"), sem("ws_masked")
        w_hi_ready, w_lo_ready = sem("w_hi_ready"), sem("w_lo_ready")
        gemm_done, evacuated = sem("gemm_done"), sem("evacuated")
        h_hi_ready, h_ready = sem("h_hi_ready"), sem("h_ready")
        squared, sum_added = sem("squared"), sem("sum_added")
        stats_done, root_ready, rstd_ready = sem("stats_done"), sem("root_ready"), sem("rstd_ready")
        gelu_done = sem("gelu_done")
        va_turned, va_copied, vb_turned, vb_copied = sem("va_turned"), sem("va_copied"), sem("vb_turned"), sem("vb_copied")
        ln_stats, ln_var_ready, ln_root, va_step = sem("ln_stats"), sem("ln_var_ready"), sem("ln_root"), sem("va_step")
        gates_done, gates_evacuated, ya_ready = sem("gates_done"), sem("gates_evacuated"), sem("ya_ready")
        mix_hi_ready, mix_ready, mix_last_ready = sem("mix_hi_ready"), sem("mix_ready"), sem("mix_last_ready")
        qk_fixed, v_fixed, skew_fixed, yb_taken = sem("qk_fixed"), sem("v_fixed"), sem("skew_fixed"), sem("yb_taken")
        half_done, half_taken = sem("half_done"), sem("half_taken")
        scores_done, near_biased, near_ready = sem("scores_done"), sem("near_biased"), sem("near_ready")
        shift_ready, exp_done, prob_step, probs_ready = sem("shift_ready"), sem("exp_done"), sem("prob_step"), sem("probs_ready")
        probs_turned, probs_t_ready, pv_done = sem("probs_turned"), sem("probs_t_ready"), sem("pv_done")
        yb_hi_ready, skew_masked, mask_set = sem("yb_hi_ready"), sem("skew_masked"), sem("mask_set")
        silu_done, product_ready, act_hi_ready, act_ready = sem("silu_done"), sem("product_ready"), sem("act_hi_ready"), sem("act_ready")
        sigmoid_done, tap_done, conv_done, z_cleared = sem("sigmoid_done"), sem("tap_done"), sem("conv_done"), sem("z_cleared")
        cln_sums, cln_mean, cln_centred, cln_squared = sem("cln_sums"), sem("cln_mean"), sem("cln_centred"), sem("cln_squared")
        cln_root, cln_scaled, cln_silu, cln_step = sem("cln_root"), sem("cln_scaled"), sem("cln_silu"), sem("cln_step")
        conv_sum = sem("conv_sum")
        s_hi_ready, s_ready = sem("s_hi_ready"), sem("s_ready")
        out_ready, out_stored = sem("out_ready"), sem("out_stored")

        def keys(t):
            tiles = min(t + 1, 5)
            near = min(tiles, 2) * P
            return tiles, near, tiles * P - near

        START = 1

        c_out = IN_CHUNKS
        at_chunk = c_out + 8
        ffn_at = []
        c_conv = c_proj = 0
        for layer in range(2):
            if layer == 1:
                c_conv, c_proj = at_chunk, at_chunk + 16
                at_chunk += 24
            groups, f0 = [], 0
            for g in GROUPS:
                groups.append((at_chunk, at_chunk + 2 * g, g, f0))
                at_chunk += 2 * g + 8
                f0 += g
            ffn_at.append(groups)
        chunks = at_chunk
        mask_q = small[0:1, 9:10]

        mask_row = at("mask_row", [1, P], CON + 2816)
        block = ctx.enter_context(nc.Block())

        @block.sync
        def _(sp):
            def load_pairs(c0, first, pairs, src):
                with sp.Fori(first, pairs) as r:
                    i = sp.snap(r)
                    for j in range(PAIR):
                        sp.wait_ge(w_lo_ready, i * PAIR + (c0 + j - 1))
                        s = src(i, j)
                        sp.dma_start(raw[:, j, 0:s.shape[-1]], s).then_inc(raw_loaded[j], 16)

            sp.dma_start(chan[:, :], per_channel).then_inc(chan_loaded, 16)
            for n in range(NT):
                sp.dma_start(xt[:, n, :], x[n]).then_inc(x_loaded[n], 16)
                if n == 1:
                    for j in range(PAIR):
                        sp.dma_start(raw[:, j, :], w_in[j]).then_inc(raw_loaded[j], 16)
            sp.dma_start(ws[:, :, :], w_ws.rearrange("j h i -> j h i")).then_inc(tables_loaded, 16)
            sp.dma_start(lng[:, :], bass.AP(tensor=ln_g.tensor, offset=0, ap=[[0, P], [1, 512]])).then_inc(tables_loaded, 16)
            sp.dma_start(lnb[:, :], bass.AP(tensor=ln_b.tensor, offset=0, ap=[[0, P], [1, 512]])).then_inc(tables_loaded, 16)
            for hh in range(2):
                sp.dma_start(bsb[64 * hh:64 * hh + 64, :, :],
                             bass.AP(tensor=b_bs.tensor, offset=hh * P, ap=[[0, HD], [2 * P, 4], [1, P]])).then_inc(tables_loaded, 16)
            sp.dma_start(far, bass.AP(tensor=rel_far.tensor, offset=0, ap=[[0, P], [1, HEADS]])).then_inc(tables_loaded, 16)

            sp.dma_start(rel_rows, bass.AP(tensor=rel_ext.tensor, offset=0, ap=[[0, P], [1, HEADS * EXT]])).then_inc(rel_spread, 16)

            load_pairs(0, 1, PRE_CHUNKS // PAIR, lambda i, j: w_in[i * PAIR + j])
            sp.wait_ge(rel_spread, 16)
            sp.wait_ge(gates_done, 4)
            sp.wait_ge(va_step, 24)
            sp.dma_start(skew[:, :, :], bass.AP(tensor=rel_rows.tensor, offset=P - 1, ap=[[HEADS * EXT - 1, P], [EXT, HEADS], [1, SKEW]])
                         ).then_inc(skew_loaded, 16)
            load_pairs(0, PRE_CHUNKS // PAIR, IN_CHUNKS // PAIR, lambda i, j: w_in[i * PAIR + j])
            load_pairs(c_out, 0, NT // PAIR, lambda i, j: w_out[i * PAIR + j])
            for layer in range(2):
                if layer == 1:
                    load_pairs(c_conv, 0, 2 * NT // PAIR, lambda i, j: w_c1[i * PAIR + j])
                    load_pairs(c_proj, 0, NT // PAIR, lambda i, j: w_c2[i * PAIR + j])
                for c_up, c_dn, g, f0 in ffn_at[layer]:
                    load_pairs(c_up, 0, 2 * g // PAIR, lambda i, j: w_gu[layer, i * PAIR + (2 * f0 + j)])
                    load_pairs(c_dn, 0, NT // PAIR, lambda i, j: w_dn[layer, i * PAIR + j, :, f0 * P:(f0 + g) * P])
            for n in range(NT):
                sp.wait_ge(out_ready, n + 1)
                sp.dma_start(out[n], o_fin[:, n, :]).then_inc(out_stored, 16)
            sp.wait_ge(out_stored, 16 * NT)

        @block.gpsimd
        def _(pool):
            pool.memset(ones[:, :], 1.0).then_inc(consts_set, 1)
            pool.memset(eps, EPS).then_inc(eps_set, 1)
            pool.memset(ident[:, :], 0.0).then_inc(ident_set, 1)
            pool.wait_ge(ident_set, 1)
            pool.affine_select(out=ident[:, :], in_=ident[:, :], compare_op=ALU.not_equal, fill=1.0, base=0,
                               pattern=[[-1, P]], channel_multiplier=1).then_inc(ident_set, 1)
            pool.memset(mask_row[:, 0:64], 0.0).then_inc(mask_set, 1)
            pool.memset(mask_row[:, 64:P], NEG).then_inc(mask_set, 1)

            def split_low(first, last):
                with pool.Fori(first, last) as i:
                    for j in range(PAIR):
                        pool.wait_ge(w_hi_ready, i * PAIR + (j + 1))
                        pool.tensor_tensor(w_lo[:, j, :], raw[:, j, :], w_hi[:, j, :].bitcast(F32), ALU.subtract
                                           ).then_inc(w_lo_ready, 1)

            split_low(0, (IN_CHUNKS + 2) // PAIR)
            for n in range(NT - 1):
                pool.wait_ge(mix_hi_ready, n + 1)
                y = au[:, 4 + n, :] if n < 4 else yb[:, n - 4, :]
                pool.tensor_tensor(p_lo[:, n, :], y, p_hi[:, n, :].bitcast(F32), ALU.subtract).then_inc(mix_ready, 1)
            split_low((IN_CHUNKS + 2) // PAIR, chunks // PAIR)

        @block.tensor
        def _(pe):
            def product(j, k, m_hi, m_lo, tiles, bank, halves=(0, 1)):
                hi, lo = (w[:, j % 2, k * P:(k + 1) * P] for w in (w_hi, w_lo))
                for n, (w, m) in enumerate(((hi, m_hi), (hi, m_lo), (lo, m_hi))):
                    for half in halves:
                        last = pe.matmul(ps[:, bank(half), :], w, m[:, k, half * HALF:(half + 1) * HALF],
                                         start=(k == 0 and n == 0), stop=(k == tiles - 1 and n == 2))
                return last

            def chunk(c, j, m_hi, m_lo, tiles, ready=None, free=None):
                pe.wait_ge(w_lo_ready, c + 1)
                if type(c) is not int or c >= QUAD:
                    pe.wait_ge(evacuated, c - 3)
                if free is not None:
                    pe.wait_ge(*free)
                for k in range(tiles):
                    if ready is not None:
                        pe.wait_ge(*ready(k))
                    last = product(j, k, m_hi, m_lo, tiles, lambda half: 2 * j + half)
                last.then_inc(gemm_done, 1)

            def quad(c, m_hi, m_lo, tiles, ready=None, free=None, stats=None):
                for j in range(QUAD):
                    if j == 3 and stats is not None:
                        pe.wait_ge(root_ready, stats + 1)
                    chunk(c + j, j, m_hi, m_lo, tiles, ready if j == 0 else None, free(j) if free else None)
                    if j == 0 and stats is not None:
                        norm_stats(stats)

            def quads(c0, n, m_hi, m_lo, tiles, ready, stats=None):
                first = 0
                if stats is not None:
                    quad(c0, m_hi, m_lo, tiles, ready, stats=stats)
                    first = 1
                with pe.Fori(first, n) as i:
                    quad(i * QUAD + c0, m_hi, m_lo, tiles, ready)

            def norm_stats(k):
                pe.wait_ge(sum_added, 9 * (k + 1))
                for half in range(2):
                    last = pe.matmul(ps[:, 6 + half, :], ones[:, :], sumsq[:, half * HALF:(half + 1) * HALF], start=True, stop=True)
                last.then_inc(stats_done, 1)

            def h_of(k):
                return lambda t: (h_ready, NT * k + t + 1)

            pe.sem_inc(pv_done, START)
            pe.sem_inc(probs_turned, PROBS)
            pe.wait_ge(consts_set, 1)
            quads(0, 2, p_hi, p_lo, NT, h_of(0), stats=0)
            pe.wait_ge(ident_set, 2)
            pe.wait_ge(gelu_done, 4)
            pe.wait_ge(evacuated, 8)
            for b in range(8):
                for m in range(4):
                    last = pe.transpose(ps[:, b, m * P:(m + 1) * P], au[:, m, b * P:(b + 1) * P], ident[:, :])
                last.then_inc(va_turned, 1)
            quad(8, p_hi, p_lo, NT, free=lambda j: (va_copied, 2 * j + 2))
            pe.wait_ge(va_step, 24)
            pe.wait_ge(ws_masked, 1)
            for m in range(4):
                pe.wait_ge(evacuated, 9 + m)
                for b in range(8):
                    for hh in range(2):
                        h = 2 * m + hh
                        last = pe.matmul(ps[64 * hh:64 * hh + 64, 2 * m + b // 4, (b % 4) * P:(b % 4 + 1) * P],
                                         va_tok[:, b, h * HD:(h + 1) * HD], ws[:, h, :], start=True, stop=True)
                last.then_inc(gates_done, 1)
            for j in range(2):
                chunk(12 + j, j, p_hi, p_lo, NT, free=(gates_evacuated, j + 1))
            for n, b in enumerate((4, 5, 6, 7, 0, 1, 2, 3)):
                if n == 0:
                    pe.wait_ge(gates_evacuated, 4)
                elif n >= 4:
                    pe.wait_ge(evacuated, 13 + b // 2)
                for m in range(4):
                    last = pe.transpose(ps[:, b, m * P:(m + 1) * P], vb[:, m, b * P:(b + 1) * P], ident[:, :])
                last.then_inc(vb_turned, 1)
            pe.wait_ge(mask_set, 2)
            pe.wait_ge(vb_copied, 8)

            def scores(m, u):
                t, hh = u // 2, u % 2
                rows = slice(64 * hh, 64 * hh + 64)
                tiles, near, farther = keys(t)
                k0 = (t + 1 - tiles) * P
                if type(m) is not int or m > 0:
                    if u == 0:
                        pe.wait_ge(qk_fixed, m * 4 + 2)
                    if u == 6:
                        pe.wait_ge(qk_fixed, m * 4 + 4)
                if type(m) is not int or m * UNITS + u >= 2:
                    pe.wait_ge(exp_done, m * UNITS + (u - 1) + START)
                query = q_fix[rows, t * P:(t + 1) * P]
                if farther:
                    far_at = HALF - farther
                    pe.matmul(pair(hh)[:, far_at:HALF], query, k_fix[rows, k0:k0 + farther], start=True, stop=(t < 4))
                    if t >= 4:
                        pe.matmul(pair(hh)[:, far_at:far_at + 64], mask_row[:, :], ones[0:1, 0:64], start=False, stop=True)
                pe.matmul(pair(hh)[:, HALF:HALF + near], query, k_fix[rows, k0 + farther:k0 + farther + near],
                          start=True, stop=True).then_inc(scores_done, 1)

            def turn(m, u):
                pe.wait_ge(probs_ready, m * UNITS + (u + 1))
                pe.wait_ge(probs_t_ready, START + m * UNITS + u)
                for k in range(keys(u // 2)[0]):
                    last = pe.transpose(ps[:, 4 + k // 4, (k % 4) * P:(k % 4 + 1) * P], probs[:, u % PROBS, k * P:(k + 1) * P], ident[:, :])
                last.then_inc(probs_turned, 1)

            def values(m, u, final):
                t, hh = u // 2, u % 2
                tiles = keys(t)[0]
                b0 = t + 1 - tiles
                pe.wait_ge(probs_t_ready, START + m * UNITS + (u + 1))
                if u == 0:
                    pe.wait_ge(v_fixed, m * 2 + 1)
                if u == 6:
                    pe.wait_ge(v_fixed, m * 2 + 2)
                if hh == 0 and final and t >= 1:
                    pe.wait_ge(mix_last_ready, t)
                elif hh == 0:
                    pe.wait_ge(yb_taken, m * 8 + (t + 1))
                for k in range(tiles):
                    last = pe.matmul(ps[64 * hh:64 * hh + 64, 6, 0:P], v_fix[:, b0 + k, 64 * hh:64 * hh + 64],
                                     probs_t[:, k * P:(k + 1) * P], start=(k == 0), stop=(k == tiles - 1))
                last.then_inc(pv_done, 1)

            def heads(m, final):
                filled = 0
                for s in range(UNITS):
                    if not final:
                        for _ in range(FILL[s]):
                            n, k = filled // NT, filled % NT
                            j, half = n // 2, n % 2
                            if k == 0:
                                pe.wait_ge(half_taken, START + m * 4 + n)
                                pe.wait_ge(w_lo_ready, m * 2 + (PRE_CHUNKS + j + 1))
                            last = product(j, k, p_hi, p_lo, NT, lambda _: 7, (half,))
                            if k == NT - 1:
                                last.then_inc(half_done, 1)
                            filled += 1
                    values(m, s, final)
                    if s + 1 < UNITS:
                        turn(m, s + 1)
                    elif not final:
                        turn(m + 1, 0)
                    if s + AHEAD < UNITS:
                        scores(m, s + AHEAD)
                    elif not final:
                        scores(m + 1, s + AHEAD - UNITS)

            for u in range(AHEAD):
                scores(0, u)
            turn(0, 0)
            with pe.Fori(0, 3) as m:
                heads(m, False)
            heads(3, True)
            pe.sem_inc(gemm_done, IN_CHUNKS - PRE_CHUNKS)
            quad(c_out, p_hi, p_lo, NT, lambda k: (mix_last_ready, 8) if k == NT - 1 else (mix_ready, k + 1))
            quad(c_out + QUAD, p_hi, p_lo, NT)
            for layer in range(2):
                if layer == 1:
                    quads(c_conv, 4, q_hi, q_lo, NT, h_of(2), stats=2)
                    pe.wait_ge(evacuated, c_proj)
                    pe.wait_ge(conv_sum, NT + 1)
                    for half in range(2):
                        last = pe.matmul(ps[:, half, :], ones[:, :], sumsq[:, half * HALF:(half + 1) * HALF], start=True, stop=True)
                    last.then_inc(cln_sums, 1)
                    pe.wait_ge(cln_squared, NT + 1)
                    for half in range(2):
                        last = pe.matmul(ps[:, half, :], ones[:, :], sumsq[:, half * HALF:(half + 1) * HALF], start=True, stop=True)
                    last.then_inc(cln_sums, 1)
                    pe.wait_ge(cln_root, 1)
                    quads(c_proj, 2, p_hi, p_lo, NT, lambda k: (s_ready, k + 1))
                done = FT * layer
                for n, (c_up, c_dn, g, f0) in enumerate(ffn_at[layer]):
                    norm = 1 + 2 * layer
                    quads(c_up, 2 * g // QUAD, q_hi, q_lo, NT, h_of(norm), stats=norm if n == 0 else None)
                    base = done + f0
                    quads(c_dn, 2, p_hi, p_lo, g, lambda k: (act_ready, START + base + k + 1))
            norm_stats(4)

        @block.scalar
        def _(se):
            def apart():
                se.wait_ge(eps_set, 1)

            def split_ahead(c, j, read=None):
                s = j % PAIR
                if type(c) is int and c + 2 >= chunks:
                    return
                q = c + (2 - s)
                se.wait_ge(raw_loaded[s], q * 8 + 16)
                if type(c) is not int or c >= 0:
                    se.wait_ge(*(read or (gemm_done, c + 1)))
                se.activation(w_hi[:, s, :], raw[:, s, :], ACT.Copy).then_inc(w_hi_ready, 1)

            def quads(c0, n, work=None, tail=False):
                def body(i, c):
                    for j in range(QUAD):
                        split_ahead(c + j, j)
                        if work is not None:
                            work(i, j, c + j)
                with se.Fori(0, n - 1 if tail else n) as i:
                    body(i, i * QUAD + c0)
                if tail:
                    body(n - 1, (n - 1) * QUAD + c0)

            def prepare(k, n, gain, hi, split=True):
                se.wait_ge(sum_added, n + (9 * k + 1))
                if type(n) is not int:
                    apart()
                if split:
                    se.activation(hi[:, n, :], xt[:, n, :], ACT.Copy, scale=gain).then_inc(h_hi_ready, 1)
                se.activation(square[:, :], xt[:, n, :], ACT.Square).then_inc(squared, 1)

            def root(k):
                se.wait_ge(stats_done, k + 1)
                se.activation(rstd[:, :], pair(3), ACT.Sqrt, bias=eps, scale=1.0 / D).then_inc(root_ready, 1)

            def gain(name, n):
                return chan[:, bass.ds(n + COLS[name], 1)]

            se.sem_inc(exp_done, START)
            se.sem_inc(probs_t_ready, START)
            se.wait_ge(chan_loaded, 16)
            for n in range(NT):
                se.wait_ge(x_loaded[n], 16)
                prepare(0, n, gain("g_mix", n), p_hi)
                if n == 1:
                    split_ahead(-2, 2)
                    split_ahead(-1, 3)
            se.wait_ge(eps_set, 1)
            root(0)

            def gelu(i, j, c):
                se.wait_ge(evacuated, c + 1)
                tile = au[:, i * QUAD + j, :]
                apart()
                se.activation(tile, tile, ACT.Gelu_apprx_tanh).then_inc(gelu_done, 1)

            quads(0, 2, gelu)
            for b in range(8):
                se.wait_ge(va_turned, b + 1)
                se.activation(va_tok[:, b, :], ps[:, b, :], ACT.Copy).then_inc(va_copied, 1)
            se.wait_ge(ln_stats, 16)
            se.activation(small[:, 32:40], small[:, 16:32].rearrange("p (b s) -> p b s", s=2)[:, :, 1], ACT.Sqrt, bias=eps
                          ).then_inc(ln_root, 1)
            quads(8, 1)
            for j in range(2):
                split_ahead(12 + j, j)
            for n, b in enumerate((4, 5, 6, 7, 0, 1, 2, 3)):
                se.wait_ge(vb_turned, n + 1)
                se.activation(vb_tok[:, b, :], ps[:, b, :], ACT.Copy).then_inc(vb_copied, 1)

            def exps(m, u):
                tiles, near, farther = keys(u // 2)
                s = 40 + 8 * (u % 2)
                se.wait_ge(probs_turned, m * UNITS + (u + 1))
                se.wait_ge(shift_ready, m * UNITS + (u + 1))
                se.activation(probs[:, u % PROBS, 0:tiles * P], pair(u % 2)[:, HALF - farther:HALF + near], ACT.Exp,
                              bias=small[:, s + 2:s + 3], accum_out=small[:, s + 3:s + 4]).then_inc(exp_done, 1)

            def copy_turned(m, u):
                n = keys(u // 2)[0] * P
                se.wait_ge(probs_turned, m * UNITS + (u + 1 + PROBS))
                se.wait_ge(pv_done, START + m * UNITS + u)
                se.activation(probs_t[:, 0:n], pair(2)[:, 0:n], ACT.Copy).then_inc(probs_t_ready, 1)

            def y_high(t):
                se.wait_ge(pv_done, START + 3 * UNITS + (2 * t + 2))
                se.activation(p_hi[:, 7, t * P:(t + 1) * P], ps[:, 6, 0:P], ACT.Copy).then_inc(yb_hi_ready, 1)

            def heads(m, final):
                for s in range(UNITS):
                    if final and s % 2:
                        y_high(s // 2)
                    if s + 1 < UNITS:
                        copy_turned(m, s + 1)
                    elif not final:
                        copy_turned(m + 1, 0)
                    if s + AHEAD < UNITS:
                        exps(m, s + AHEAD)
                    elif not final:
                        exps(m + 1, s + AHEAD - UNITS)
                    if not final and s in (4, 9):
                        j = s // 9
                        split_ahead(m * 2 + (PRE_CHUNKS + j), j, (half_done, m * 4 + (2 * j + 2)))
                    if final and s % 2 and s // 2 < 7:
                        n = s // 2
                        se.wait_ge(ya_ready, 4)
                        se.wait_ge(half_done, 12)
                        se.wait_ge(yb_taken, START + 3 * 8)
                        se.activation(p_hi[:, n, :], au[:, 4 + n, :] if n < 4 else yb[:, n - 4, :], ACT.Copy).then_inc(mix_hi_ready, 1)

            for u in range(AHEAD):
                exps(0, u)
            copy_turned(0, 0)
            with se.Fori(0, 3) as m:
                heads(m, False)
            heads(3, True)

            def down(k, name, hi):
                def work(i, j, c):
                    se.wait_ge(evacuated, c + 1)
                    n = i * QUAD + j
                    prepare(k, n, gain(name, n + (8 if name == "g_mix" or k == 3 else 0)), hi, split=k < 4)
                return work

            quads(c_out, 2, down(1, "g_ffn", q_hi))
            for layer in range(2):
                if layer == 1:
                    root(2)

                    def sigmoid(i, j, c):
                        if j % 2:
                            n = i * 2 + j // 2
                            se.wait_ge(evacuated, c + 1)
                            apart()
                            se.activation(act[:, :], up[:, :], ACT.Sigmoid, bias=gain("c_b1", n + 8)).then_inc(sigmoid_done, 1)
                    quads(c_conv, 4, sigmoid)
                    se.wait_ge(cln_sums, 1)
                    se.activation(mean_b[:, :], pair(0), ACT.Copy, scale=1.0 / D).then_inc(cln_mean, 1)
                    for n in range(NT):
                        se.wait_ge(cln_centred, n + 1)
                        se.wait_ge(cln_squared, n + 1)
                        se.activation(square[:, :], y_even[:, n, :], ACT.Square).then_inc(cln_step, 1)
                    se.wait_ge(cln_sums, 2)
                    se.activation(mean_b[:, :], pair(0), ACT.Sqrt, bias=eps, scale=1.0 / D).then_inc(cln_root, 1)
                    for n in range(NT):
                        se.wait_ge(cln_scaled, n + 2)
                        buf = (gate, up)[n % 2]
                        se.activation(buf[:, :], buf[:, :], ACT.Silu, scale=gain("c_ln_g", n), bias=gain("c_ln_b", n)).then_inc(cln_silu, 1)
                        se.wait_ge(cln_silu, n + 1)
                        se.activation(p_hi[:, n, :], buf[:, :], ACT.Copy).then_inc(s_hi_ready, 1)
                    quads(c_proj, 2, down(3, "g_ffn", q_hi))
                norm = 1 + 2 * layer
                root(norm)
                for n, (c_up, c_dn, g, f0) in enumerate(ffn_at[layer]):
                    base = FT * layer + f0

                    def inner(i, j, c):
                        f = i * 2 + (base + j // 2)
                        if j % 2 == 0:
                            se.wait_ge(evacuated, c + 1)
                            se.wait_ge(product_ready, START + f)
                            se.activation(act[:, :], gate[:, :], ACT.Silu).then_inc(silu_done, 1)
                        else:
                            se.wait_ge(product_ready, START + f + 1)
                            apart()
                            se.activation(p_hi[:, i * 2 + j // 2, :], up[:, :], ACT.Copy).then_inc(act_hi_ready, 1)
                    quads(c_up, 2 * g // QUAD, inner)
                    last = n == len(GROUPS) - 1
                    work = down(2 + 2 * layer, "g_mix", q_hi) if last else None
                    quads(c_dn, 2, work, tail=last and layer == 1)
            root(4)

        @block.vector
        def _(ve):
            def evacuate(c, j, dst, factor=None):
                ve.wait_ge(gemm_done, c + 1)
                if factor is None:
                    ve.tensor_tensor(dst, pair(j), rstd[:, :], ALU.mult).then_inc(evacuated, 1)
                else:
                    ve.scalar_tensor_tensor(out=dst, in0=pair(j), scalar=factor, in1=rstd[:, :], op0=ALU.mult, op1=ALU.mult
                                            ).then_inc(evacuated, 1)

            def quads(c0, n, work):
                with ve.Fori(0, n) as i:
                    for j in range(QUAD):
                        work(i, j, i * QUAD + (c0 + j))

            def clear_sum(k):
                if k:
                    ve.wait_ge(stats_done, k)
                ve.memset(sumsq[:, :], 0.0).then_inc(sum_added, 1)

            def prepare(k, n, gain, hi, lo, split=True):
                if split:
                    ve.wait_ge(h_hi_ready, n + (NT * k + 1))
                    ve.scalar_tensor_tensor(out=lo[:, n, :], in0=xt[:, n, :], scalar=gain, in1=hi[:, n, :].bitcast(F32),
                                            op0=ALU.mult, op1=ALU.subtract).then_inc(h_ready, 1)
                ve.wait_ge(squared, n + (NT * k + 1))
                ve.wait_ge(sum_added, n + (9 * k + 1))
                ve.tensor_tensor(sumsq[:, :], sumsq[:, :], square[:, :], ALU.add).then_inc(sum_added, 1)

            def invert(k):
                ve.wait_ge(root_ready, k + 1)
                ve.reciprocal(rstd[:, :], rstd[:, :]).then_inc(rstd_ready, 1)
                ve.wait_ge(rstd_ready, k + 1)

            def gain(name, n):
                return chan[:, bass.ds(n + COLS[name], 1)]

            for counted in (product_ready, act_ready, tap_done):
                ve.sem_inc(counted, START)
            ve.sem_inc(yb_taken, START)
            ve.sem_inc(half_taken, START)
            ve.sem_inc(qk_fixed, 4)
            clear_sum(0)
            ve.wait_ge(chan_loaded, 16)
            for n in range(NT):
                ve.wait_ge(x_loaded[n], 16)
                prepare(0, n, gain("g_mix", n), p_hi, p_lo)
            ve.wait_ge(tables_loaded, 16 * 6)
            ve.memset(ws[64:P, :, 0:64], 0.0).then_inc(ws_masked, 1)
            invert(0)
            quads(0, 2, lambda i, j, c: evacuate(c, j, au[:, i * QUAD + j, :]))
            for b in range(8):
                ve.wait_ge(va_copied, b + 1)
                ve.bn_stats(square[:, 6 * b:6 * b + 6], va_tok[:, b, :]).then_inc(ln_stats, 1)
            ve.wait_ge(ln_stats, 8)
            for b in range(8):
                ve.bn_aggr(small[:, 16 + 2 * b:18 + 2 * b], square[:, 6 * b:6 * b + 6]).then_inc(ln_stats, 1)
            ve.wait_ge(ln_root, 1)
            ve.reciprocal(small[:, 32:40], small[:, 32:40]).then_inc(ln_var_ready, 1)
            ve.wait_ge(ln_var_ready, 1)
            ve.wait_ge(ln_stats, 16)
            for b in range(8):
                ve.tensor_scalar(va_tok[:, b, :], va_tok[:, b, :], small[:, 16 + 2 * b:17 + 2 * b], small[:, 32 + b:33 + b],
                                 ALU.subtract, ALU.mult).then_inc(va_step, 1)
            ve.wait_ge(va_step, 8)
            for b in range(8):
                ve.tensor_tensor(va_tok[:, b, :], va_tok[:, b, :], lng[:, :], ALU.mult).then_inc(va_step, 1)
            ve.wait_ge(va_step, 16)
            for b in range(8):
                ve.tensor_tensor(va_tok[:, b, :], va_tok[:, b, :], lnb[:, :], ALU.add).then_inc(va_step, 1)
            for j in range(QUAD):
                evacuate(8 + j, j, vb[:, j, :])
            for m in range(4):
                buf = (square, sumsq)[m % 2]
                ve.wait_ge(gates_done, m + 1)
                ve.tensor_tensor(buf[:, :].rearrange("p (b i) -> p b i", i=P), pair(m).rearrange("p (b i) -> p b i", i=P),
                                 bass.AP(tensor=bsb[:, m, :].tensor, offset=bsb[:, m, :].offset,
                                         ap=[list(bsb[:, m, :].ap[0]), [0, 8], [1, P]]), ALU.add).then_inc(gates_evacuated, 1)
                ve.wait_ge(gates_evacuated, m + 1)
                ve.wait_ge(gelu_done, 8)
                ve.tensor_tensor(au[:, 4 + m, :], buf[:, :], au[:, 4 + m, :], ALU.mult).then_inc(ya_ready, 1)
            evacuate(12, 0, q_fix[:, :], float(HD) ** -0.5)
            ve.wait_ge(skew_loaded, 16)
            ve.memset(skew[0:64, :, SKEW - 64:SKEW], NEG).then_inc(skew_masked, 1)
            ve.wait_ge(skew_masked, 1)
            ve.tensor_tensor(skew[:, :, :], skew[:, :, :], bass.AP(tensor=far.tensor, offset=far.offset,
                             ap=[list(far.ap[0]), [1, HEADS], [0, SKEW]]), ALU.subtract).then_inc(skew_masked, 1)
            ve.wait_ge(skew_masked, 2)
            ve.wait_ge(gates_evacuated, 4)
            ve.tensor_copy(skew_fix[:, :, :], skew[:, 0:2, :]).then_inc(skew_fixed, 1)
            evacuate(13, 1, k_fix[:, :])
            ve.wait_ge(skew_fixed, 1)

            def maxima(m, u):
                t, hh = u // 2, u % 2
                tiles, near, farther = keys(t)
                s = 40 + 8 * (u % 2)
                ve.wait_ge(scores_done, m * UNITS + (u + 1))
                scored = pair(hh)[:, HALF:HALF + near]
                biases = skew_fix[:, hh, SKEW - near:SKEW]
                if farther:
                    ve.tensor_reduce(small[:, s:s + 1], pair(hh)[:, HALF - farther:HALF], AX.X, ALU.max)
                    ve.tensor_tensor_reduce(scored, scored, biases, 1.0, NEG, ALU.add, ALU.max, small[:, s + 1:s + 2]
                                            ).then_inc(near_ready, 1)
                else:
                    ve.tensor_tensor(scored, scored, biases, ALU.add).then_inc(near_biased, 1)
                    ve.wait_ge(near_biased, m * 4 + (u + 1))
                    ve.tensor_reduce(small[:, s + 1:s + 2], scored, AX.X, ALU.max).then_inc(near_ready, 1)

            def shift(m, u):
                s = 40 + 8 * (u % 2)
                ve.wait_ge(near_ready, m * UNITS + (u + 1))
                if u >= 4:
                    ve.tensor_scalar(small[:, s + 2:s + 3], small[:, s:s + 1], small[:, s + 1:s + 2], -1.0, ALU.max, ALU.mult
                                     ).then_inc(shift_ready, 1)
                else:
                    ve.tensor_scalar(small[:, s + 2:s + 3], small[:, s + 1:s + 2], -1.0, None, ALU.mult).then_inc(shift_ready, 1)

            def invert_sum(m, u):
                s = 40 + 8 * (u % 2)
                ve.wait_ge(exp_done, START + m * UNITS + (u + 1))
                ve.reciprocal(small[:, s + 4:s + 5], small[:, s + 3:s + 4]).then_inc(prob_step, 1)

            def normalise(m, u):
                s = 40 + 8 * (u % 2)
                n = keys(u // 2)[0] * P
                ve.wait_ge(prob_step, m * UNITS + (u + 1))
                ve.tensor_scalar(probs[:, u % PROBS, 0:n], probs[:, u % PROBS, 0:n], small[:, s + 4:s + 5], None, ALU.mult
                                 ).then_inc(probs_ready, 1)

            def softmax(m, u, more=True):
                at_m, at_u = (m, u) if u < UNITS else (m + 1, u - UNITS)
                before = (m, u - 1) if u - 1 < UNITS else (m + 1, u - 1 - UNITS)
                if more:
                    maxima(at_m, at_u)
                if u >= 1:
                    invert_sum(*before)
                if more:
                    shift(at_m, at_u)
                if u >= 1:
                    normalise(*before)

            def copy_v(m, first, last):
                ve.tensor_copy(v_fix[:, first:last, :], vb_tok[:, first:last, bass.ds(m * P, P)] if type(m) is not int else
                               vb_tok[:, first:last, m * P:(m + 1) * P]).then_inc(v_fixed, 1)

            def heads(m, final):
                for s in range(UNITS):
                    u = s + AHEAD
                    if s % 2:
                        t = s // 2
                        cols = slice(t * P, (t + 1) * P)
                        if final:
                            ve.wait_ge(yb_hi_ready, t + 1)
                            ve.tensor_tensor(p_lo[:, 7, cols], ps[:, 6, 0:P], p_hi[:, 7, cols].bitcast(F32), ALU.subtract
                                             ).then_inc(mix_last_ready, 1)
                        else:
                            ve.wait_ge(pv_done, START + m * UNITS + (s + 1))
                            ve.tensor_scalar(yb[:, m, cols], ps[:, 6, 0:P], 1.0, None, ALU.mult).then_inc(yb_taken, 1)
                    if not final and s in HALF_ENDS:
                        n = HALF_ENDS.index(s)
                        cols = slice(n % 2 * HALF, (n % 2 + 1) * HALF)
                        ve.wait_ge(half_done, m * 4 + (n + 1))
                        if n == 0:
                            ve.wait_ge(qk_fixed, m * 4 + 4)
                        if n < 2:
                            ve.scalar_tensor_tensor(out=q_next[:, cols], in0=ps[:, 7, :], scalar=float(HD) ** -0.5, in1=rstd[:, cols],
                                                    op0=ALU.mult, op1=ALU.mult).then_inc(half_taken, 1)
                        else:
                            ve.tensor_tensor(k_next[:, cols], ps[:, 7, :], rstd[:, cols], ALU.mult).then_inc(half_taken, 1)
                    if u <= UNITS or not final:
                        softmax(m, u, not final or u < UNITS)
                    if final:
                        continue
                    if s == 10:
                        ve.wait_ge(half_taken, START + m * 4 + 4)
                        ve.wait_ge(scores_done, m * UNITS + 14)
                        ve.tensor_copy(q_fix[:, 0:7 * P], q_next[:, 0:7 * P]).then_inc(qk_fixed, 1)
                        ve.tensor_copy(k_fix[:, 0:3 * P], k_next[:, 0:3 * P]).then_inc(qk_fixed, 1)
                    if s == 11:
                        ve.wait_ge(scores_done, m * UNITS + 16)
                        ve.tensor_copy(q_fix[:, 7 * P:T], q_next[:, 7 * P:T]).then_inc(qk_fixed, 1)
                        ve.tensor_copy(k_fix[:, 3 * P:T], k_next[:, 3 * P:T]).then_inc(qk_fixed, 1)
                        ve.wait_ge(near_ready, m * UNITS + 16)
                        ve.tensor_copy(skew_fix[:, :, :], skew[:, bass.ds(m * 2 + 2, 2), :]).then_inc(skew_fixed, 1)
                        ve.wait_ge(skew_fixed, m + 2)
                    if s == 14:
                        ve.wait_ge(pv_done, START + m * UNITS + 14)
                        copy_v(m + 1, 0, 3)
                    if s == 15:
                        ve.wait_ge(pv_done, START + m * UNITS + 16)
                        copy_v(m + 1, 3, 8)

            for u in range(AHEAD):
                softmax(0, u)
                if u == 1:
                    ve.wait_ge(vb_copied, 8)
                    copy_v(0, 0, 3)
                    copy_v(0, 3, 8)
            with ve.Fori(0, 3) as m:
                heads(m, False)
            heads(3, True)

            def down(k, name, bias=None):
                def work(i, j, c):
                    n = i * QUAD + j
                    ve.wait_ge(gemm_done, c + 1)
                    if bias is None:
                        ve.tensor_tensor(xt[:, n, :], pair(j), xt[:, n, :], ALU.add).then_inc(evacuated, 1)
                    else:
                        ve.scalar_tensor_tensor(out=xt[:, n, :], in0=pair(j), scalar=gain(bias, n), in1=xt[:, n, :],
                                                op0=ALU.add, op1=ALU.add).then_inc(evacuated, 1)
                    if k is not None:
                        ve.wait_ge(evacuated, c + 1)
                        prepare(k, n, gain(name, n + (8 if name == "g_mix" or k == 3 else 0)), q_hi, q_lo, split=k < 4)
                return work

            ve.sem_inc(evacuated, IN_CHUNKS - PRE_CHUNKS)
            clear_sum(1)
            quads(c_out, 2, down(1, "g_ffn"))
            for layer in range(2):
                if layer == 1:
                    invert(2)
                    ve.memset(z_pad[:, 0:PAD], 0.0).then_inc(z_cleared, 1)
                    ve.wait_ge(z_cleared, 1)
                    ve.wait_ge(stats_done, 3)
                    ve.memset(sumsq[:, :], 0.0).then_inc(conv_sum, 1)
                    TAPS = CONV_W + 2

                    def conv(i, j, c):
                        n = i * 2 + j // 2
                        if j % 2 == 0:
                            ve.wait_ge(tap_done, START + n * TAPS)
                            evacuate(c, j, gate[:, :])
                            return
                        evacuate(c, j, up[:, :])
                        ve.wait_ge(sigmoid_done, n + 1)
                        ve.scalar_tensor_tensor(out=z_pad[:, PAD:PAD + T], in0=gate[:, :], scalar=gain("c_b1", n), in1=act[:, :],
                                                op0=ALU.add, op1=ALU.mult).then_inc(tap_done, 1)
                        ve.wait_ge(tap_done, START + n * TAPS + 1)

                        def tap(k):
                            return chan[:, bass.ds(n * CONV_W + (COLS["c_dw"] + k), 1)]
                        ve.tensor_scalar(y_even[:, n, :], z_pad[:, 0:T], tap(0), gain("c_bdw", n), ALU.mult, ALU.add).then_inc(tap_done, 1)
                        ve.tensor_scalar(y_odd[:, :], z_pad[:, 1:1 + T], tap(1), None, ALU.mult).then_inc(tap_done, 1)
                        for k in range(2, CONV_W):
                            y = y_odd[:, :] if k % 2 else y_even[:, n, :]
                            ve.wait_ge(tap_done, START + n * TAPS + k)
                            ve.scalar_tensor_tensor(out=y, in0=z_pad[:, k:k + T], scalar=tap(k), in1=y, op0=ALU.mult, op1=ALU.add
                                                    ).then_inc(tap_done, 1)
                        ve.wait_ge(tap_done, START + n * TAPS + (CONV_W + 1))
                        ve.tensor_tensor(y_even[:, n, :], y_even[:, n, :], y_odd[:, :], ALU.add).then_inc(tap_done, 1)
                        ve.wait_ge(tap_done, START + n * TAPS + (CONV_W + 2))
                        ve.wait_ge(conv_sum, n + 1)
                        ve.tensor_tensor(sumsq[:, :], sumsq[:, :], y_even[:, n, :], ALU.add).then_inc(conv_sum, 1)
                    quads(c_conv, 4, conv)
                    ve.wait_ge(cln_mean, 1)
                    ve.memset(sumsq[:, :], 0.0).then_inc(cln_squared, 1)
                    for n in range(NT):
                        ve.tensor_tensor(y_even[:, n, :], y_even[:, n, :], mean_b[:, :], ALU.subtract).then_inc(cln_centred, 1)
                    for n in range(NT):
                        ve.wait_ge(cln_step, n + 1)
                        ve.wait_ge(cln_squared, n + 1)
                        ve.tensor_tensor(sumsq[:, :], sumsq[:, :], square[:, :], ALU.add).then_inc(cln_squared, 1)
                    ve.wait_ge(cln_root, 1)
                    ve.reciprocal(mean_b[:, :], mean_b[:, :]).then_inc(cln_scaled, 1)
                    ve.wait_ge(cln_scaled, 1)

                    def conv_low(n):
                        ve.wait_ge(s_hi_ready, n + 1)
                        buf = (gate, up)[n % 2]
                        ve.tensor_tensor(p_lo[:, n, :], buf[:, :], p_hi[:, n, :].bitcast(F32), ALU.subtract).then_inc(s_ready, 1)

                    for n in range(NT):
                        if n >= 2:
                            conv_low(n - 2)
                            ve.wait_ge(s_ready, n - 1)
                        buf = (gate, up)[n % 2]
                        ve.tensor_tensor(buf[:, :], y_even[:, n, :], mean_b[:, :], ALU.mult).then_inc(cln_scaled, 1)
                    conv_low(NT - 2)
                    conv_low(NT - 1)
                    ve.wait_ge(cln_sums, 2)
                    clear_sum(3)
                    quads(c_proj, 2, down(3, "g_ffn", bias="c_b2"))
                norm = 1 + 2 * layer
                invert(norm)
                clear_sum(2 + 2 * layer)
                for n, (c_up, c_dn, g, f0) in enumerate(ffn_at[layer]):
                    base = FT * layer + f0

                    def inner(i, j, c):
                        f = i * 2 + (base + j // 2)
                        if j % 2 == 0:
                            evacuate(c, j, gate[:, :])
                            return
                        ve.wait_ge(act_ready, START + f)
                        evacuate(c, j, up[:, :])
                        ve.wait_ge(silu_done, f + 1)
                        ve.wait_ge(evacuated, c + 1)
                        ve.tensor_tensor(up[:, :], up[:, :], act[:, :], ALU.mult).then_inc(product_ready, 1)
                        ve.wait_ge(act_hi_ready, f + 1)
                        k = i * 2 + j // 2
                        ve.tensor_tensor(p_lo[:, k, :], up[:, :], p_hi[:, k, :].bitcast(F32), ALU.subtract).then_inc(act_ready, 1)
                    quads(c_up, 2 * g // QUAD, inner)
                    last = n == len(GROUPS) - 1
                    quads(c_dn, 2, down(2 + 2 * layer if last else None, "g_mix"))
            invert(4)
            for n in range(NT):
                ve.scalar_tensor_tensor(out=o_fin[:, n, :], in0=xt[:, n, :], scalar=gain("g_final", n), in1=rstd[:, :],
                                        op0=ALU.mult, op1=ALU.mult).then_inc(out_ready, 1)


def kernel(x, w_in, w_out, a_ln_g, a_ln_b, a_ws, a_bs, b_rel, c_w1, c_b1, c_dw, c_bdw, c_ln_g, c_ln_b, c_w2, c_b2,
           g_mix, g_ffn, f_wg, f_wu, f_wd, g_final):
    import numpy as np
    import concourse.bacc as bacc
    from concourse import mybir as mb
    from concourse.bass_utils import run_bass_kernel_spmd

    def by_chunk(w):
        w = np.asarray(w)
        k, n = w.shape
        return w.reshape(k // P, P, n // P, P).transpose(2, 1, 0, 3).reshape(n // P, P, k)

    def by_partition(v):
        v = np.asarray(v)
        return v.reshape(-1, P).T

    wi = by_chunk(w_in[0])
    order = [4, 5, 6, 7, 0, 1, 2, 3, 16, 17, 18, 19, 8, 12, 9, 13, 10, 14, 11, 15]
    c1 = by_chunk(c_w1[0])
    rel = np.asarray(b_rel)[0][:, ::-1]
    ext = np.concatenate([np.broadcast_to(rel[:, :1], (HEADS, P - 1)), rel[:, :EXT - P + 1]], axis=1)
    dw = np.asarray(c_dw)[0].T.reshape(NT, P, CONV_W).transpose(1, 0, 2).reshape(P, NT * CONV_W)
    arrays = {
        "x": np.asarray(x)[0].T.reshape(NT, P, T),
        "w_in": wi[order],
        "w_out": by_chunk(w_out[0]),
        "w_ws": np.asarray(a_ws)[0].transpose(2, 0, 1),
        "b_bs": np.asarray(a_bs)[0],
        "ln_g": np.asarray(a_ln_g),
        "ln_b": np.asarray(a_ln_b),
        "rel_ext": ext,
        "rel_far": rel[:, :1].reshape(1, HEADS),
        "per_channel": np.concatenate([by_partition(v) for v in (g_mix, g_ffn, g_final, c_b1, c_bdw, c_ln_g, c_ln_b, c_b2)] + [dw], axis=1),
        "w_c1": np.stack([c1[:NT], c1[NT:]], axis=1).reshape(2 * NT, P, D),
        "w_c2": by_chunk(c_w2[0]),
        "w_gu": np.stack([np.stack([by_chunk(f_wg[n]), by_chunk(f_wu[n])], axis=1).reshape(2 * FT, P, D) for n in range(2)]),
        "w_dn": np.stack([by_chunk(f_wd[n]) for n in range(2)]),
    }
    arrays = {k: np.ascontiguousarray(v) for k, v in arrays.items()}
    nc = bacc.Bacc("TRN2", target_bir_lowering=False, num_devices=1, dynamic_dma_scratch_size=DMA_RING)
    args = {k: nc.dram_tensor(f"in_{k}", v.shape, mb.dt.from_np(v.dtype), kind="ExternalInput").ap() for k, v in arrays.items()}
    args["out"] = nc.dram_tensor("out", (NT, P, T), mb.dt.float32, kind="ExternalOutput").ap()
    build(nc, **args)
    r = run_bass_kernel_spmd(nc, [{f"in_{k}": v for k, v in arrays.items()}], core_ids=[0])
    return np.ascontiguousarray(r.results[0]["out"].reshape(D, T).T).reshape(1, T, D)
```

```python
from contextlib import ExitStack

import concourse.bass as bass
from concourse import mybir

F32 = mybir.dt.float32
F32R = mybir.dt.float32r
ALU = mybir.AluOpType
ACT = mybir.ActivationFunctionType
AX = mybir.AxisListType

P = 128
T = 1024
D = 1024
NT = D // P
HALF = 512
HEADS = 8
HD = 64
D_FF = 2816
FT = D_FF // P
GROUPS = (8, 8, 6)
CONV_W = 31
PAD = CONV_W - 1
POOL_TAPS = (0, 8) + (10,) * (NT - 3) + (7,)
PE_TAPS = (0,) * (NT - 2) + (12, 10)
EPS = 1e-6
NEG = -1e30
QUAD = 4
PAIR = 2
BAND = 640
SKEW = 256
EXT = 384
PROBS = 4
UNITS = 16
AHEAD = 4
FILL = (4, 4, 4, 4, 3, 3, 2, 3, 3, 2) + (0,) * 6
HALF_ENDS = (1, 3, 6, 9)

DMA_RING = 1024
SBUF_FREE = DMA_RING + 128
IN_CHUNKS = 20
PRE_CHUNKS = 14
COLS = {}
_at = 0
for _name, _n in (("g_mix", 16), ("g_ffn", 16), ("g_final", 8), ("c_b1", 16), ("c_bdw", 8), ("c_ln_g", 8),
                  ("c_ln_b", 8), ("c_b2", 8), ("c_dw", 8 * CONV_W)):
    COLS[_name] = _at
    _at += _n
N_COLS = _at


def build(nc, x, w_in, w_out, w_ws, b_bs, ln_g, ln_b, rel_ext, rel_far, per_channel, w_c1, w_c2, w_gu, w_dn, out):
    ctx = ExitStack()
    with ctx:
        K = 1024
        X0, PH, PL, RAW, WH, WL, RS, CON, ARENA = (SBUF_FREE + n for n in (
            0, 32 * K, 64 * K, 96 * K, 112 * K, 120 * K, 128 * K, 132 * K, 132 * K + 3328))
        QH, QL, TMP = ARENA, ARENA + 32 * K, ARENA + 64 * K

        def at(name, shape, offset, dt=F32):
            return nc.alloc_sbuf_tensor_at(name, shape, dt, offset=offset)

        xt = at("xt", [P, NT, T], X0)
        p_hi = at("p_hi", [P, NT, T], PH, F32R)
        p_lo = at("p_lo", [P, NT, T], PL, F32R)
        q_hi = at("q_hi", [P, NT, T], QH, F32R)
        q_lo = at("q_lo", [P, NT, T], QL, F32R)
        raw = at("raw", [P, PAIR, NT * P], RAW)
        w_hi = at("w_hi", [P, 2, NT * P], WH, F32R)
        w_lo = at("w_lo", [P, 2, NT * P], WL, F32R)
        rstd = at("rstd", [P, T], RS)
        chan = at("chan", [P, N_COLS], CON)
        ones = at("ones", [P, P], CON + 1536)
        ident = at("ident", [P, P], CON + 2048)
        small = at("small", [P, 64], CON + 2560)
        eps = small[:, 0:1]
        far = small[:, 1:9]
        assert N_COLS * 4 <= 1536
        au = at("au", [P, 8, T], QH)
        vb_tok = at("vb_tok", [P, 8, 512], QH)
        vb = at("vb", [P, 4, T], QL)
        va_tok = at("va_tok", [P, 8, 512], QL + 16 * K)
        ws = at("ws", [P, HEADS, P], TMP)
        lng = at("lng", [P, 512], TMP + 4 * K)
        lnb = at("lnb", [P, 512], TMP + 6 * K)
        bsb = at("bsb", [P, 4, P], TMP + 8 * K)
        skew = at("skew", [P, HEADS, SKEW], TMP)
        q_fix = at("q_fix", [P, T], QL + 16 * K)
        k_fix = at("k_fix", [P, T], QL + 20 * K)
        v_fix = at("v_fix", [P, 8, P], QL + 24 * K)
        q_next = at("q_next", [P, T], QL + 28 * K)
        k_next = at("k_next", [P, T], QL + 12 * K)
        yb = at("yb", [P, 3, T], QL)
        probs_t = at("probs_t", [P, BAND], TMP + 20 * K)
        skew_fix = at("skew_fix", [P, 2, SKEW], TMP + 8 * K)
        probs = at("probs", [P, PROBS, BAND], TMP + 10 * K)
        sumsq = at("sumsq", [P, T], TMP + 10 * K)
        square = at("square", [P, T], TMP + 14 * K)
        gate = at("gate", [P, T], TMP)
        up = at("up", [P, T], TMP + 4 * K)
        act = at("act", [P, T], TMP + 18 * K)
        z_pad = [at(f"z_pad{n}", [P, T + PAD], PH + 4352 * n) for n in range(2)]
        pool_sum = [at(f"pool_sum{n}", [P, T], PH + (9 + 4 * n) * K) for n in range(2)]
        scaled = [at(f"scaled{n}", [P, T], PH + (17 + 4 * n) * K) for n in range(3)]
        diagonals = at("diagonals", [P, 8, P], TMP + 14 * K)
        y = at("y", [P, NT, T], PL)
        centred_sq = at("centred_sq", [P, NT, T], PH)
        tap_diagonals = [at("tap_diagonals0", [P, 16, P], TMP + 10 * K), at("tap_diagonals1", [P, 16, P], RAW + 8 * K)]
        silus = (gate, up, act, sumsq)
        o_fin = at("o_fin", [P, NT, T], PH)

        ps = nc.alloc_psum_tensor("ps", [P, 8, HALF], F32)

        def pair(j):
            return ps[:, 2 * j:2 * j + 2, :].rearrange("p a n -> p (a n)")


        rel_rows = nc.dram_tensor("rel_rows", (P, HEADS * EXT), F32, kind="Internal").ap()

        def sem(name):
            return nc.alloc_semaphore(name)

        x_loaded = [sem(f"x_loaded{n}") for n in range(NT)]
        chan_loaded, tables_loaded, rel_spread, skew_loaded = sem("chan_loaded"), sem("tables_loaded"), sem("rel_spread"), sem("skew_loaded")
        raw_loaded = [sem(f"raw_loaded{s}") for s in range(PAIR)]
        consts_set, ident_set, eps_set, ws_masked = sem("consts_set"), sem("ident_set"), sem("eps_set"), sem("ws_masked")
        w_hi_ready, w_lo_ready = sem("w_hi_ready"), sem("w_lo_ready")
        gemm_done, evacuated = sem("gemm_done"), sem("evacuated")
        h_hi_ready, h_ready = sem("h_hi_ready"), sem("h_ready")
        squared, sum_added = sem("squared"), sem("sum_added")
        stats_done, root_ready, rstd_ready = sem("stats_done"), sem("root_ready"), sem("rstd_ready")
        gelu_done = sem("gelu_done")
        va_turned, va_copied, vb_turned, vb_copied = sem("va_turned"), sem("va_copied"), sem("vb_turned"), sem("vb_copied")
        ln_stats, ln_var_ready, ln_root, va_step = sem("ln_stats"), sem("ln_var_ready"), sem("ln_root"), sem("va_step")
        gates_done, gates_evacuated, ya_ready = sem("gates_done"), sem("gates_evacuated"), sem("ya_ready")
        mix_hi_ready, mix_ready, mix_last_ready = sem("mix_hi_ready"), sem("mix_ready"), sem("mix_last_ready")
        qk_fixed, v_fixed, skew_fixed, yb_taken = sem("qk_fixed"), sem("v_fixed"), sem("skew_fixed"), sem("yb_taken")
        half_done, half_taken = sem("half_done"), sem("half_taken")
        scores_done, near_biased, near_ready = sem("scores_done"), sem("near_biased"), sem("near_ready")
        shift_ready, exp_done, prob_step, probs_ready = sem("shift_ready"), sem("exp_done"), sem("prob_step"), sem("probs_ready")
        probs_turned, probs_t_ready, pv_done = sem("probs_turned"), sem("probs_t_ready"), sem("pv_done")
        yb_hi_ready, skew_masked, mask_set = sem("yb_hi_ready"), sem("skew_masked"), sem("mask_set")
        silu_done, product_ready, act_hi_ready, act_ready = sem("silu_done"), sem("product_ready"), sem("act_hi_ready"), sem("act_ready")
        sigmoid_done, tap_done, z_cleared = sem("sigmoid_done"), sem("tap_done"), sem("z_cleared")
        cln_sums, cln_centred, cln_added, cln_added_pool = sem("cln_sums"), sem("cln_centred"), sem("cln_added"), sem("cln_added_pool")
        cln_scaled, cln_silu, cln_step = sem("cln_scaled"), sem("cln_silu"), sem("cln_step")
        diagonals_set, pe_taps_done = sem("diagonals_set"), sem("pe_taps_done")
        z_ready, tap_scaled, tap_folded = sem("z_ready"), sem("tap_scaled"), sem("tap_folded")
        column_sums, column_root, column_step, rows_ready = sem("column_sums"), sem("column_root"), sem("column_step"), sem("rows_ready")
        s_hi_ready, s_even_ready, s_odd_ready = sem("s_hi_ready"), sem("s_even_ready"), sem("s_odd_ready")
        out_ready, out_stored = sem("out_ready"), sem("out_stored")

        def before(n, counts):
            return sum(counts[:n]) if type(n) is int else n * counts[2] + (sum(counts[:2]) - 2 * counts[2])

        def scaled_before(n):
            return before(n, POOL_TAPS)

        def folded_before(n):
            return before(n, [max(taps - 1, 0) for taps in POOL_TAPS])

        VE_TAPS = [CONV_W - a - b for a, b in zip(POOL_TAPS, PE_TAPS)]

        def taps_before(n):
            return before(n, [taps + 1 for taps in VE_TAPS])

        def conv_pairs(body, pe_like):
            body(0)
            with pe_like.Fori(1, NT // 2 - 1) as i:
                body(i)
            body(NT // 2 - 1)

        def keys(t):
            tiles = min(t + 1, 5)
            near = min(tiles, 2) * P
            return tiles, near, tiles * P - near

        def place(m, u):
            t = u // 2
            return (9 - t if type(m) is int and m == 3 and u >= 4 else t), u % 2

        START = 1

        c_out = IN_CHUNKS
        at_chunk = c_out + 8
        ffn_at = []
        c_conv = c_proj = 0
        for layer in range(2):
            if layer == 1:
                c_conv, c_proj = at_chunk, at_chunk + 16
                at_chunk += 24
            groups, f0 = [], 0
            for g in GROUPS:
                groups.append((at_chunk, at_chunk + 2 * g, g, f0))
                at_chunk += 2 * g + 8
                f0 += g
            ffn_at.append(groups)
        chunks = at_chunk

        mask_row = at("mask_row", [1, P], CON + 2816)
        block = ctx.enter_context(nc.Block())

        @block.sync
        def _(sp):
            def load_pairs(c0, first, pairs, src):
                with sp.Fori(first, pairs) as r:
                    i = sp.snap(r)
                    for j in range(PAIR):
                        sp.wait_ge(w_lo_ready, i * PAIR + (c0 + j - 1))
                        s = src(i, j)
                        sp.dma_start(raw[:, j, 0:s.shape[-1]], s).then_inc(raw_loaded[j], 16)

            sp.dma_start(raw[:, 0, :], w_in[0]).then_inc(raw_loaded[0], 16)
            sp.dma_start(chan[:, :], per_channel).then_inc(chan_loaded, 16)
            for n in range(NT):
                sp.dma_start(xt[:, n, :], x[n]).then_inc(x_loaded[n], 16)
                if n == 3:
                    sp.dma_start(raw[:, 1, :], w_in[1]).then_inc(raw_loaded[1], 16)
            load_pairs(0, 1, 2, lambda i, j: w_in[i * PAIR + j])
            sp.dma_start(ws[:, :, :], w_ws.rearrange("j h i -> j h i")).then_inc(tables_loaded, 16)
            sp.dma_start(lng[:, :], bass.AP(tensor=ln_g.tensor, offset=0, ap=[[0, P], [1, 512]])).then_inc(tables_loaded, 16)
            sp.dma_start(lnb[:, :], bass.AP(tensor=ln_b.tensor, offset=0, ap=[[0, P], [1, 512]])).then_inc(tables_loaded, 16)
            for hh in range(2):
                sp.dma_start(bsb[64 * hh:64 * hh + 64, :, :],
                             bass.AP(tensor=b_bs.tensor, offset=hh * P, ap=[[0, HD], [2 * P, 4], [1, P]])).then_inc(tables_loaded, 16)
            sp.dma_start(far, bass.AP(tensor=rel_far.tensor, offset=0, ap=[[0, P], [1, HEADS]])).then_inc(tables_loaded, 16)

            sp.dma_start(rel_rows, bass.AP(tensor=rel_ext.tensor, offset=0, ap=[[0, P], [1, HEADS * EXT]])).then_inc(rel_spread, 16)

            load_pairs(0, 2, PRE_CHUNKS // PAIR, lambda i, j: w_in[i * PAIR + j])
            sp.wait_ge(rel_spread, 16)
            sp.wait_ge(gates_done, 4)
            sp.wait_ge(va_step, 24)
            sp.dma_start(skew[:, :, :], bass.AP(tensor=rel_rows.tensor, offset=P - 1, ap=[[HEADS * EXT - 1, P], [EXT, HEADS], [1, SKEW]])
                         ).then_inc(skew_loaded, 16)
            load_pairs(0, PRE_CHUNKS // PAIR, IN_CHUNKS // PAIR, lambda i, j: w_in[i * PAIR + j])
            load_pairs(c_out, 0, NT // PAIR, lambda i, j: w_out[i * PAIR + j])
            for layer in range(2):
                if layer == 1:
                    load_pairs(c_conv, 0, 2 * NT // PAIR, lambda i, j: w_c1[i * PAIR + j])
                    load_pairs(c_proj, 0, NT // PAIR, lambda i, j: w_c2[i * PAIR + j])
                for c_up, c_dn, g, f0 in ffn_at[layer]:
                    load_pairs(c_up, 0, 2 * g // PAIR, lambda i, j: w_gu[layer, i * PAIR + (2 * f0 + j)])
                    load_pairs(c_dn, 0, NT // PAIR, lambda i, j: w_dn[layer, i * PAIR + j, :, f0 * P:(f0 + g) * P])
            for n in range(NT):
                sp.wait_ge(out_ready, n + 1)
                sp.dma_start(out[n], o_fin[:, n, :]).then_inc(out_stored, 16)
            sp.wait_ge(out_stored, 16 * NT)

        @block.gpsimd
        def _(pool):
            pool.memset(ones[:, :], 1.0).then_inc(consts_set, 1)
            pool.memset(eps, EPS).then_inc(eps_set, 1)
            pool.memset(ident[:, :], 0.0).then_inc(ident_set, 1)
            pool.wait_ge(ident_set, 1)
            pool.affine_select(out=ident[:, :], in_=ident[:, :], compare_op=ALU.not_equal, fill=1.0, base=0,
                               pattern=[[-1, P]], channel_multiplier=1).then_inc(ident_set, 1)
            pool.memset(mask_row[:, 0:64], 0.0).then_inc(mask_set, 1)
            pool.memset(mask_row[:, 64:P], NEG).then_inc(mask_set, 1)

            def low(c, s):
                pool.wait_ge(w_hi_ready, c + 1)
                pool.tensor_tensor(w_lo[:, s, :], raw[:, s, :], w_hi[:, s, :].bitcast(F32), ALU.subtract).then_inc(w_lo_ready, 1)

            def split_low(first, last):
                with pool.Fori(first, last) as i:
                    for j in range(PAIR):
                        low(i * PAIR + j, j)

            split_low(0, (IN_CHUNKS + 2) // PAIR)
            for n in range(NT - 1):
                pool.wait_ge(mix_hi_ready, n + 1)
                y = au[:, 4 + n, :] if n < 4 else yb[:, n - 4, :]
                pool.tensor_tensor(p_lo[:, n, :], y, p_hi[:, n, :].bitcast(F32), ALU.subtract).then_inc(mix_ready, 1)
            split_low((IN_CHUNKS + 2) // PAIR, (c_conv + 6) // PAIR)

            def conv_sums(i):
                for e in range(2):
                    n = i * 2 + e
                    peeled = type(n) is int
                    taps = POOL_TAPS[n + 1 if peeled and n + 1 < NT else 2]
                    acc = pool_sum[(e + 1) % 2]
                    splits = not peeled or n + 2 < NT
                    for k in range(1, taps if not (peeled and n + 1 >= NT) else 0):
                        if splits and k in (taps // 3, 2 * taps // 3):
                            low(n * 2 + (c_conv + 6 + (0 if k == taps // 3 else 1)), 0 if k == taps // 3 else 1)
                        if k == 1:
                            pool.wait_ge(tap_scaled, scaled_before(n + 1) + 2)
                            pool.tensor_tensor(acc[:, :], scaled[0][:, :], scaled[1][:, :], ALU.add).then_inc(tap_folded, 1)
                        else:
                            pool.wait_ge(tap_folded, folded_before(n + 1) + (k - 1))
                            pool.wait_ge(tap_scaled, scaled_before(n + 1) + (k + 1))
                            pool.tensor_tensor(acc[:, :], acc[:, :], scaled[k % 3][:, :], ALU.add).then_inc(tap_folded, 1)

            conv_pairs(conv_sums, pool)
            for n in range(1, NT // 2):
                pool.wait_ge(cln_step, n + 1)
                if n > 1:
                    pool.wait_ge(cln_added_pool, n - 1)
                pool.tensor_tensor(centred_sq[:, 0, :], centred_sq[:, 0, :], centred_sq[:, n, :], ALU.add).then_inc(cln_added_pool, 1)
            for n in range(1, NT, 2):
                pool.wait_ge(s_hi_ready, n + 1)
                pool.tensor_tensor(p_lo[:, n, :], silus[n % 4][:, :], p_hi[:, n, :].bitcast(F32), ALU.subtract).then_inc(s_odd_ready, 1)
            split_low((c_conv + 18) // PAIR, chunks // PAIR)

        @block.tensor
        def _(pe):
            def product(j, k, m_hi, m_lo, tiles, bank, halves=(0, 1)):
                hi, lo = (w[:, j % 2, k * P:(k + 1) * P] for w in (w_hi, w_lo))
                for n, (w, m) in enumerate(((hi, m_hi), (hi, m_lo), (lo, m_hi))):
                    for half in halves:
                        last = pe.matmul(ps[:, bank(half), :], w, m[:, k, half * HALF:(half + 1) * HALF],
                                         start=(k == 0 and n == 0), stop=(k == tiles - 1 and n == 2))
                return last

            def chunk(c, j, m_hi, m_lo, tiles, ready=None, free=None):
                pe.wait_ge(w_lo_ready, c + 1)
                if type(c) is not int or c >= QUAD:
                    pe.wait_ge(evacuated, c - 3)
                if free is not None:
                    pe.wait_ge(*free)
                for k in range(tiles):
                    if ready is not None:
                        pe.wait_ge(*ready(k))
                    last = product(j, k, m_hi, m_lo, tiles, lambda half: 2 * j + half)
                last.then_inc(gemm_done, 1)

            def quad(c, m_hi, m_lo, tiles, ready=None, free=None, stats=None):
                after = 1 if stats == 0 else 0
                for j in range(QUAD):
                    if j == 3 and stats is not None:
                        pe.wait_ge(root_ready, stats + 1)
                    chunk(c + j, j, m_hi, m_lo, tiles, ready if j == 0 else None, free(j) if free else None)
                    if j == after and stats is not None:
                        norm_stats(stats)

            def quads(c0, n, m_hi, m_lo, tiles, ready, stats=None):
                first = 0
                if stats is not None:
                    quad(c0, m_hi, m_lo, tiles, ready, stats=stats)
                    first = 1
                with pe.Fori(first, n) as i:
                    quad(i * QUAD + c0, m_hi, m_lo, tiles, ready)

            def norm_stats(k):
                pe.wait_ge(sum_added, 9 * (k + 1))
                for half in range(2):
                    last = pe.matmul(ps[:, 6 + half, :], ones[:, :], sumsq[:, half * HALF:(half + 1) * HALF], start=True, stop=True)
                last.then_inc(stats_done, 1)

            def h_of(k):
                return lambda t: (h_ready, NT * k + t + 1)

            def sum_columns(tile):
                for b in range(8):
                    last = pe.matmul(ps[:, 6, b:b + 1], tile[:, b * P:(b + 1) * P], ones[:, 0:1], start=True, stop=True)
                last.then_inc(column_sums, 1)

            def spread(r):
                for b in range(8):
                    pe.wait_ge(column_step, r * 9 + b + 2)
                    last = pe.matmul(ps[:, 4 + b // 4, (b % 4) * P:(b % 4 + 1) * P], ones[:, :], diagonals[:, b, :], start=True, stop=True)
                last.then_inc(rows_ready, 1)

            pe.sem_inc(pv_done, START)
            pe.sem_inc(probs_turned, PROBS)
            pe.wait_ge(consts_set, 1)
            quads(0, 2, p_hi, p_lo, NT, h_of(0), stats=0)
            pe.wait_ge(ident_set, 2)
            pe.wait_ge(gelu_done, 4)
            pe.wait_ge(evacuated, 8)
            for b in range(8):
                for m in range(4):
                    last = pe.transpose(ps[:, b, m * P:(m + 1) * P], au[:, m, b * P:(b + 1) * P], ident[:, :])
                last.then_inc(va_turned, 1)
            quad(8, p_hi, p_lo, NT, free=lambda j: (va_copied, 2 * j + 2))
            pe.wait_ge(va_step, 24)
            pe.wait_ge(ws_masked, 1)
            for m in range(4):
                pe.wait_ge(evacuated, 9 + m)
                for b in range(8):
                    for hh in range(2):
                        h = 2 * m + hh
                        last = pe.matmul(ps[64 * hh:64 * hh + 64, 2 * m + b // 4, (b % 4) * P:(b % 4 + 1) * P],
                                         va_tok[:, b, h * HD:(h + 1) * HD], ws[:, h, :], start=True, stop=True)
                last.then_inc(gates_done, 1)
            for j in range(2):
                chunk(12 + j, j, p_hi, p_lo, NT, free=(gates_evacuated, j + 1))
            for n, b in enumerate((4, 5, 6, 7, 0, 1, 2, 3)):
                if n == 0:
                    pe.wait_ge(gates_evacuated, 4)
                elif n >= 4:
                    pe.wait_ge(evacuated, 13 + b // 2)
                for m in range(4):
                    last = pe.transpose(ps[:, b, m * P:(m + 1) * P], vb[:, m, b * P:(b + 1) * P], ident[:, :])
                last.then_inc(vb_turned, 1)
            pe.wait_ge(mask_set, 2)
            pe.wait_ge(vb_copied, 8)

            def scores(m, u):
                t, hh = place(m, u)
                rows = slice(64 * hh, 64 * hh + 64)
                tiles, near, farther = keys(t)
                k0 = (t + 1 - tiles) * P
                if type(m) is not int or m > 0:
                    if u == 0:
                        pe.wait_ge(qk_fixed, m * 4 + 2)
                    if u == (4 if type(m) is int and m == 3 else 6):
                        pe.wait_ge(qk_fixed, m * 4 + 4)
                if type(m) is not int or m * UNITS + u >= 2:
                    pe.wait_ge(exp_done, m * UNITS + (u - 1) + START)
                query = q_fix[rows, t * P:(t + 1) * P]
                if farther:
                    far_at = HALF - farther
                    pe.matmul(pair(hh)[:, far_at:HALF], query, k_fix[rows, k0:k0 + farther], start=True, stop=(t < 4))
                    if t >= 4:
                        pe.matmul(pair(hh)[:, far_at:far_at + 64], mask_row[:, :], ones[0:1, 0:64], start=False, stop=True)
                pe.matmul(pair(hh)[:, HALF:HALF + near], query, k_fix[rows, k0 + farther:k0 + farther + near],
                          start=True, stop=True).then_inc(scores_done, 1)

            def turn(m, u):
                pe.wait_ge(probs_ready, m * UNITS + (u + 1))
                pe.wait_ge(probs_t_ready, START + m * UNITS + u)
                for k in range(keys(place(m, u)[0])[0]):
                    last = pe.transpose(ps[:, 4 + k // 4, (k % 4) * P:(k % 4 + 1) * P], probs[:, u % PROBS, k * P:(k + 1) * P], ident[:, :])
                last.then_inc(probs_turned, 1)

            def values(m, u, final):
                t, hh = place(m, u)
                tiles = keys(t)[0]
                b0 = t + 1 - tiles
                pe.wait_ge(probs_t_ready, START + m * UNITS + (u + 1))
                if u == 0:
                    pe.wait_ge(v_fixed, m * 2 + 1)
                if u == (4 if type(m) is int and m == 3 else 6):
                    pe.wait_ge(v_fixed, m * 2 + 2)
                if hh == 0 and final and u >= 2:
                    pe.wait_ge(mix_last_ready, u // 2)
                elif hh == 0:
                    pe.wait_ge(yb_taken, m * 8 + (u // 2 + 1))
                for k in range(tiles):
                    last = pe.matmul(ps[64 * hh:64 * hh + 64, 6, 0:P], v_fix[:, b0 + k, 64 * hh:64 * hh + 64],
                                     probs_t[:, k * P:(k + 1) * P], start=(k == 0), stop=(k == tiles - 1))
                last.then_inc(pv_done, 1)

            def heads(m, final):
                filled = 0
                for s in range(UNITS):
                    if not final:
                        for _ in range(FILL[s]):
                            n, k = filled // NT, filled % NT
                            j, half = n // 2, n % 2
                            if k == 0:
                                pe.wait_ge(half_taken, START + m * 4 + n)
                                pe.wait_ge(w_lo_ready, m * 2 + (PRE_CHUNKS + j + 1))
                            last = product(j, k, p_hi, p_lo, NT, lambda _: 7, (half,))
                            if k == NT - 1:
                                last.then_inc(half_done, 1)
                            filled += 1
                    values(m, s, final)
                    if s + 1 < UNITS:
                        turn(m, s + 1)
                    elif not final:
                        turn(m + 1, 0)
                    if s + AHEAD < UNITS:
                        scores(m, s + AHEAD)
                    elif not final:
                        scores(m + 1, s + AHEAD - UNITS)

            for u in range(AHEAD):
                scores(0, u)
            turn(0, 0)
            with pe.Fori(0, 3) as m:
                heads(m, False)
            heads(3, True)
            pe.sem_inc(gemm_done, IN_CHUNKS - PRE_CHUNKS)
            quad(c_out, p_hi, p_lo, NT, lambda k: (mix_last_ready, 8) if k == NT - 1 else (mix_ready, k + 1))
            quad(c_out + QUAD, p_hi, p_lo, NT)
            for layer in range(2):
                if layer == 1:
                    def conv_chunk(c, j, ready=None):
                        pe.wait_ge(w_lo_ready, c + 1)
                        pe.wait_ge(evacuated, c - 1)
                        for k in range(NT):
                            if ready is not None:
                                pe.wait_ge(*ready(k))
                            last = product(j, k, q_hi, q_lo, NT, lambda half: 2 * j + half)
                        last.then_inc(gemm_done, 1)

                    def conv_total(n, first=False, last=False):
                        pe.wait_ge(tap_done, START + taps_before(n + 1))
                        for half in range(2):
                            step = pe.matmul(ps[:, half, :], ones[:, :], y[:, n, half * HALF:(half + 1) * HALF], start=first, stop=last)
                        if last:
                            step.then_inc(cln_sums, 1)

                    conv_chunk(c_conv, 0, h_of(2))
                    norm_stats(2)
                    for c in range(1, 4):
                        conv_chunk(c_conv + c, c % 2)
                    pe.wait_ge(root_ready, 3)

                    def conv_step(i):
                        for e in range(2):
                            n = i * 2 + e
                            peeled = type(n) is int
                            if not peeled or n + 2 < NT:
                                conv_chunk(n * 2 + (c_conv + 4), 0)
                            if not peeled or n + 2 < NT:
                                conv_chunk(n * 2 + (c_conv + 5), 1)

                    conv_pairs(conv_step, pe)

                    def conv_taps(n, into):
                        e, taps = n % 2, PE_TAPS[n]
                        pe.wait_ge(evacuated, c_conv + 2 * (NT - 1) + into + 1)
                        pe.wait_ge(z_ready, START + n + 1)
                        pe.wait_ge(diagonals_set, sum(PE_TAPS[:n + 1]))
                        for k in range(taps):
                            for half in range(2):
                                at_z = VE_TAPS[n] + k + half * HALF
                                last = pe.matmul(ps[:, 2 * into + half, :], tap_diagonals[e][:, k, :], z_pad[e][:, at_z:at_z + HALF],
                                                 start=(k == 0), stop=(k == taps - 1))
                        last.then_inc(pe_taps_done, 1)

                    conv_taps(NT - 2, 0)
                    conv_taps(NT - 1, 1)
                    pe.wait_ge(tap_done, START + taps_before(NT - 2) + 2)
                    pe.wait_ge(evacuated, c_proj)
                    for n in range(NT):
                        conv_total(n, first=n == 0, last=n == NT - 1)
                    pe.wait_ge(cln_added, 4)
                    sum_columns(centred_sq[:, 4, :])
                    spread(0)
                    quads(c_proj, 2, p_hi, p_lo, NT, lambda k: ((s_even_ready, s_odd_ready)[k % 2], k // 2 + 1))
                done = FT * layer
                for n, (c_up, c_dn, g, f0) in enumerate(ffn_at[layer]):
                    norm = 1 + 2 * layer
                    quads(c_up, 2 * g // QUAD, q_hi, q_lo, NT, h_of(norm), stats=norm if n == 0 else None)
                    base = done + f0
                    quads(c_dn, 2, p_hi, p_lo, g, lambda k: (act_ready, START + base + k + 1))
            pe.wait_ge(sum_added, 9 * 5)
            sum_columns(sumsq[:, :])
            spread(1)

        @block.scalar
        def _(se):
            def apart():
                se.wait_ge(eps_set, 1)

            def split_ahead(c, j, read=None):
                s = j % PAIR
                if type(c) is int and c + 2 >= chunks:
                    return
                q = c + (2 - s)
                se.wait_ge(raw_loaded[s], q * 8 + 16)
                if type(c) is not int or c >= 0:
                    se.wait_ge(*(read or (gemm_done, c + 1)))
                se.activation(w_hi[:, s, :], raw[:, s, :], ACT.Copy).then_inc(w_hi_ready, 1)

            def quads(c0, n, work=None, tail=False):
                def body(i, c):
                    for j in range(QUAD):
                        split_ahead(c + j, j)
                        if work is not None:
                            work(i, j, c + j)
                with se.Fori(0, n - 1 if tail else n) as i:
                    body(i, i * QUAD + c0)
                if tail:
                    body(n - 1, (n - 1) * QUAD + c0)

            def prepare(k, n, gain, hi, split=True, square_too=True):
                if not square_too:
                    se.activation(hi[:, n, :], xt[:, n, :], ACT.Copy, scale=gain).then_inc(h_hi_ready, 1)
                    return
                se.wait_ge(sum_added, n + (9 * k + 1))
                if type(n) is not int:
                    apart()
                if split:
                    se.activation(hi[:, n, :], xt[:, n, :], ACT.Copy, scale=gain).then_inc(h_hi_ready, 1)
                se.activation(square[:, :], xt[:, n, :], ACT.Square).then_inc(squared, 1)

            def root_of_columns(r):
                se.wait_ge(column_sums, r + 1)
                se.activation(small[:, 32:40], ps[:, 6, 0:8], ACT.Sqrt, bias=eps, scale=1.0 / D).then_inc(column_root, 1)

            def root(k):
                se.wait_ge(stats_done, k + 1)
                se.activation(rstd[:, :], pair(3), ACT.Sqrt, bias=eps, scale=1.0 / D).then_inc(root_ready, 1)

            def gain(name, n):
                return chan[:, bass.ds(n + COLS[name], 1)]

            se.sem_inc(exp_done, START)
            se.sem_inc(probs_t_ready, START)
            split_ahead(-2, 0)
            se.wait_ge(chan_loaded, 16)
            for n in range(NT):
                se.wait_ge(x_loaded[n], 16)
                prepare(0, n, gain("g_mix", n), p_hi, square_too=False)
                if n == 3:
                    split_ahead(-1, 1)
            for n in range(NT):
                if n:
                    se.wait_ge(sum_added, n)
                se.activation((square, rstd)[n % 2][:, :], xt[:, n, :], ACT.Square).then_inc(squared, 1)
                if n == 4:
                    split_ahead(0, 0)
            se.wait_ge(sum_added, 9)
            se.wait_ge(eps_set, 1)
            root(0)
            split_ahead(1, 1)

            def gelu(i, j, c):
                se.wait_ge(evacuated, c + 1)
                tile = au[:, i * QUAD + j, :]
                apart()
                se.activation(tile, tile, ACT.Gelu_apprx_tanh).then_inc(gelu_done, 1)

            for j in range(QUAD):
                if j >= 2:
                    split_ahead(j, j)
                gelu(0, j, j)
            for j in range(QUAD):
                split_ahead(QUAD + j, j)
                gelu(1, j, QUAD + j)
            for b in range(8):
                se.wait_ge(va_turned, b + 1)
                se.activation(va_tok[:, b, :], ps[:, b, :], ACT.Copy).then_inc(va_copied, 1)
            se.wait_ge(ln_stats, 16)
            se.activation(small[:, 32:40], small[:, 16:32].rearrange("p (b s) -> p b s", s=2)[:, :, 1], ACT.Sqrt, bias=eps
                          ).then_inc(ln_root, 1)
            quads(8, 1)
            for j in range(2):
                split_ahead(12 + j, j)
            for n, b in enumerate((4, 5, 6, 7, 0, 1, 2, 3)):
                se.wait_ge(vb_turned, n + 1)
                se.activation(vb_tok[:, b, :], ps[:, b, :], ACT.Copy).then_inc(vb_copied, 1)

            def exps(m, u):
                tiles, near, farther = keys(place(m, u)[0])
                s = 40 + 8 * (u % 2)
                se.wait_ge(probs_turned, m * UNITS + (u + 1))
                se.wait_ge(shift_ready, m * UNITS + (u + 1))
                se.activation(probs[:, u % PROBS, 0:tiles * P], pair(u % 2)[:, HALF - farther:HALF + near], ACT.Exp,
                              bias=small[:, s + 2:s + 3], accum_out=small[:, s + 3:s + 4]).then_inc(exp_done, 1)

            def copy_turned(m, u):
                n = keys(place(m, u)[0])[0] * P
                se.wait_ge(probs_turned, m * UNITS + (u + 1 + PROBS))
                se.wait_ge(pv_done, START + m * UNITS + u)
                se.activation(probs_t[:, 0:n], pair(2)[:, 0:n], ACT.Copy).then_inc(probs_t_ready, 1)

            def y_high(t):
                se.wait_ge(pv_done, START + 3 * UNITS + (2 * t + 2))
                t = place(3, 2 * t)[0]
                se.activation(p_hi[:, 7, t * P:(t + 1) * P], ps[:, 6, 0:P], ACT.Copy).then_inc(yb_hi_ready, 1)

            def heads(m, final):
                for s in range(UNITS):
                    if final and s % 2:
                        y_high(s // 2)
                    if s + 1 < UNITS:
                        copy_turned(m, s + 1)
                    elif not final:
                        copy_turned(m + 1, 0)
                    if s + AHEAD < UNITS:
                        exps(m, s + AHEAD)
                    elif not final:
                        exps(m + 1, s + AHEAD - UNITS)
                    if not final and s in (4, 9):
                        j = s // 9
                        split_ahead(m * 2 + (PRE_CHUNKS + j), j, (half_done, m * 4 + (2 * j + 2)))

            for u in range(AHEAD):
                exps(0, u)
            copy_turned(0, 0)
            with se.Fori(0, 3) as m:
                heads(m, False)
            heads(3, True)

            def down(k, name, hi):
                def work(i, j, c):
                    se.wait_ge(evacuated, c + 1)
                    n = i * QUAD + j
                    prepare(k, n, gain(name, n + (8 if name == "g_mix" or k == 3 else 0)), hi, split=k < 4)
                return work

            quads(c_out, 2, down(1, "g_ffn", q_hi))
            for layer in range(2):
                if layer == 1:
                    root(2)

                    def sigmoid(n):
                        se.wait_ge(evacuated, n * 2 + (c_conv + 2))
                        se.wait_ge(z_ready, START + n)
                        if type(n) is not int:
                            apart()
                        se.activation(act[:, :], up[:, :], ACT.Sigmoid, bias=gain("c_b1", n + 8)).then_inc(sigmoid_done, 1)

                    def scale_taps(n, parity, first, last, taps):
                        for k in range(first, last):
                            slot = scaled[k % 3]
                            if k == 0:
                                se.wait_ge(z_ready, START + n + 1)
                            if k < 3:
                                if type(n) is not int or n > 1:
                                    se.wait_ge(tap_folded, folded_before(n))
                            else:
                                se.wait_ge(tap_folded, folded_before(n) + (max(k - 4, 0) + 1))
                            if type(n) is not int:
                                apart()
                            weight = chan[:, bass.ds(n * CONV_W + (COLS["c_dw"] + CONV_W - taps + k), 1)]
                            at_z = CONV_W - taps + k
                            z = z_pad[parity][:, at_z:at_z + T]
                            if k == 0:
                                se.activation(slot[:, :], z, ACT.Identity, scale=weight, bias=gain("c_bdw", n)).then_inc(tap_scaled, 1)
                            else:
                                se.activation(slot[:, :], z, ACT.Copy, scale=weight).then_inc(tap_scaled, 1)

                    split_ahead(c_conv, 0)
                    for n in range(NT - 2, NT):
                        for k in range(PE_TAPS[n]):
                            tap = COLS["c_dw"] + n * CONV_W + VE_TAPS[n] + k
                            se.activation(tap_diagonals[n % 2][:, k, :], ident[:, :], ACT.Copy, scale=chan[:, tap:tap + 1]
                                          ).then_inc(diagonals_set, 1)
                    split_ahead(c_conv + 1, 1)
                    sigmoid(0)
                    split_ahead(c_conv + 2, 0)
                    split_ahead(c_conv + 3, 1)
                    sigmoid(1)

                    def conv_step(i):
                        for e in range(2):
                            n = i * 2 + e
                            peeled = type(n) is int
                            more = not peeled or n + 2 < NT
                            if peeled and n + 1 >= NT:
                                continue
                            taps = POOL_TAPS[n + 1 if peeled else 2]
                            cuts = (0, taps // 3 + 1, 2 * taps // 3 + 1, taps)
                            for part in range(3):
                                scale_taps(n + 1, (e + 1) % 2, cuts[part], cuts[part + 1], taps)
                                if more and part < 2:
                                    split_ahead(n * 2 + (c_conv + 4 + part), part)
                            if more:
                                sigmoid(n + 2)

                    conv_pairs(conv_step, se)
                    for n in range(NT):
                        se.wait_ge(cln_centred, n + 1)
                        se.activation(centred_sq[:, n, :], y[:, n, :], ACT.Square).then_inc(cln_step, 1)
                    root_of_columns(0)
                    for n in range(NT):
                        se.wait_ge(cln_scaled, n + 1)
                        buf = silus[n % 4]
                        se.activation(buf[:, :], buf[:, :], ACT.Silu, scale=gain("c_ln_g", n), bias=gain("c_ln_b", n)).then_inc(cln_silu, 1)
                        se.wait_ge(cln_silu, n + 1)
                        se.activation(p_hi[:, n, :], buf[:, :], ACT.Copy).then_inc(s_hi_ready, 1)
                    quads(c_proj, 2, down(3, "g_ffn", q_hi))
                norm = 1 + 2 * layer
                root(norm)
                for n, (c_up, c_dn, g, f0) in enumerate(ffn_at[layer]):
                    base = FT * layer + f0

                    def inner(i, j, c):
                        f = i * 2 + (base + j // 2)
                        if j % 2 == 0:
                            se.wait_ge(evacuated, c + 1)
                            se.wait_ge(product_ready, START + f)
                            se.activation(act[:, :], gate[:, :], ACT.Silu).then_inc(silu_done, 1)
                        else:
                            se.wait_ge(product_ready, START + f + 1)
                            apart()
                            se.activation(p_hi[:, i * 2 + j // 2, :], up[:, :], ACT.Copy).then_inc(act_hi_ready, 1)
                    quads(c_up, 2 * g // QUAD, inner)
                    last = n == len(GROUPS) - 1
                    work = down(2 + 2 * layer, "g_mix", q_hi) if last else None
                    quads(c_dn, 2, work, tail=last and layer == 1)
            root_of_columns(1)

        @block.vector
        def _(ve):
            def evacuate(c, j, dst, factor=None):
                ve.wait_ge(gemm_done, c + 1)
                if factor is None:
                    ve.tensor_tensor(dst, pair(j), rstd[:, :], ALU.mult).then_inc(evacuated, 1)
                else:
                    ve.scalar_tensor_tensor(out=dst, in0=pair(j), scalar=factor, in1=rstd[:, :], op0=ALU.mult, op1=ALU.mult
                                            ).then_inc(evacuated, 1)

            def quads(c0, n, work):
                with ve.Fori(0, n) as i:
                    for j in range(QUAD):
                        work(i, j, i * QUAD + (c0 + j))

            def clear_sum(k):
                if k:
                    ve.wait_ge(stats_done, k)
                ve.memset(sumsq[:, :], 0.0).then_inc(sum_added, 1)

            def low_part(k, n, gain, hi, lo):
                ve.wait_ge(h_hi_ready, n + (NT * k + 1))
                ve.scalar_tensor_tensor(out=lo[:, n, :], in0=xt[:, n, :], scalar=gain, in1=hi[:, n, :].bitcast(F32),
                                        op0=ALU.mult, op1=ALU.subtract).then_inc(h_ready, 1)

            def add_square(k, n):
                ve.wait_ge(squared, n + (NT * k + 1))
                ve.wait_ge(sum_added, n + (9 * k + 1))
                added = rstd if k == 0 and n % 2 else square
                ve.tensor_tensor(sumsq[:, :], sumsq[:, :], added[:, :], ALU.add).then_inc(sum_added, 1)

            def invert(k):
                ve.wait_ge(root_ready, k + 1)
                ve.reciprocal(rstd[:, :], rstd[:, :]).then_inc(rstd_ready, 1)
                ve.wait_ge(rstd_ready, k + 1)

            def invert_columns(r):
                ve.wait_ge(column_root, r + 1)
                ve.reciprocal(small[:, 32:40], small[:, 32:40]).then_inc(column_step, 1)
                ve.wait_ge(column_step, r * 9 + 1)
                for b in range(8):
                    ve.tensor_scalar(diagonals[:, b, :], ident[:, :], small[:, 32 + b:33 + b], None, ALU.mult).then_inc(column_step, 1)
                ve.wait_ge(rows_ready, r + 1)

            def gain(name, n):
                return chan[:, bass.ds(n + COLS[name], 1)]

            for counted in (product_ready, act_ready, tap_done, z_ready):
                ve.sem_inc(counted, START)
            ve.sem_inc(yb_taken, START)
            ve.sem_inc(half_taken, START)
            ve.sem_inc(qk_fixed, 4)
            clear_sum(0)
            ve.wait_ge(chan_loaded, 16)
            for n in range(NT):
                ve.wait_ge(x_loaded[n], 16)
                low_part(0, n, gain("g_mix", n), p_hi, p_lo)
            for n in range(NT):
                add_square(0, n)
            ve.wait_ge(tables_loaded, 16 * 6)
            ve.memset(ws[64:P, :, 0:64], 0.0).then_inc(ws_masked, 1)
            invert(0)
            quads(0, 2, lambda i, j, c: evacuate(c, j, au[:, i * QUAD + j, :]))
            for b in range(8):
                ve.wait_ge(va_copied, b + 1)
                ve.bn_stats(square[:, 6 * b:6 * b + 6], va_tok[:, b, :]).then_inc(ln_stats, 1)
            ve.wait_ge(ln_stats, 8)
            for b in range(8):
                ve.bn_aggr(small[:, 16 + 2 * b:18 + 2 * b], square[:, 6 * b:6 * b + 6]).then_inc(ln_stats, 1)
            ve.wait_ge(ln_root, 1)
            ve.reciprocal(small[:, 32:40], small[:, 32:40]).then_inc(ln_var_ready, 1)
            ve.wait_ge(ln_var_ready, 1)
            ve.wait_ge(ln_stats, 16)
            for b in range(8):
                ve.tensor_scalar(va_tok[:, b, :], va_tok[:, b, :], small[:, 16 + 2 * b:17 + 2 * b], small[:, 32 + b:33 + b],
                                 ALU.subtract, ALU.mult).then_inc(va_step, 1)
            ve.wait_ge(va_step, 8)
            for b in range(8):
                ve.tensor_tensor(va_tok[:, b, :], va_tok[:, b, :], lng[:, :], ALU.mult).then_inc(va_step, 1)
            ve.wait_ge(va_step, 16)
            for b in range(8):
                ve.tensor_tensor(va_tok[:, b, :], va_tok[:, b, :], lnb[:, :], ALU.add).then_inc(va_step, 1)
            for j in range(QUAD):
                evacuate(8 + j, j, vb[:, j, :])
            for m in range(4):
                buf = (square, sumsq)[m % 2]
                ve.wait_ge(gates_done, m + 1)
                ve.tensor_tensor(buf[:, :].rearrange("p (b i) -> p b i", i=P), pair(m).rearrange("p (b i) -> p b i", i=P),
                                 bass.AP(tensor=bsb[:, m, :].tensor, offset=bsb[:, m, :].offset,
                                         ap=[list(bsb[:, m, :].ap[0]), [0, 8], [1, P]]), ALU.add).then_inc(gates_evacuated, 1)
                ve.wait_ge(gates_evacuated, m + 1)
                ve.wait_ge(gelu_done, 8)
                ve.tensor_tensor(au[:, 4 + m, :], buf[:, :], au[:, 4 + m, :], ALU.mult).then_inc(ya_ready, 1)
            evacuate(12, 0, q_fix[:, :], float(HD) ** -0.5)
            ve.wait_ge(skew_loaded, 16)
            ve.memset(skew[0:64, :, SKEW - 64:SKEW], NEG).then_inc(skew_masked, 1)
            ve.wait_ge(skew_masked, 1)
            ve.tensor_tensor(skew[:, :, :], skew[:, :, :], bass.AP(tensor=far.tensor, offset=far.offset,
                             ap=[list(far.ap[0]), [1, HEADS], [0, SKEW]]), ALU.subtract).then_inc(skew_masked, 1)
            ve.wait_ge(skew_masked, 2)
            ve.wait_ge(gates_evacuated, 4)
            ve.tensor_copy(skew_fix[:, :, :], skew[:, 0:2, :]).then_inc(skew_fixed, 1)
            evacuate(13, 1, k_fix[:, :])
            ve.wait_ge(skew_fixed, 1)

            def maxima(m, u):
                t, hh = place(m, u)
                tiles, near, farther = keys(t)
                s = 40 + 8 * (u % 2)
                ve.wait_ge(scores_done, m * UNITS + (u + 1))
                scored = pair(hh)[:, HALF:HALF + near]
                biases = skew_fix[:, hh, SKEW - near:SKEW]
                if farther:
                    ve.tensor_reduce(small[:, s:s + 1], pair(hh)[:, HALF - farther:HALF], AX.X, ALU.max)
                    ve.tensor_tensor_reduce(scored, scored, biases, 1.0, NEG, ALU.add, ALU.max, small[:, s + 1:s + 2]
                                            ).then_inc(near_ready, 1)
                else:
                    ve.tensor_tensor(scored, scored, biases, ALU.add).then_inc(near_biased, 1)
                    ve.wait_ge(near_biased, m * 4 + (u + 1))
                    ve.tensor_reduce(small[:, s + 1:s + 2], scored, AX.X, ALU.max).then_inc(near_ready, 1)

            def shift(m, u):
                s = 40 + 8 * (u % 2)
                ve.wait_ge(near_ready, m * UNITS + (u + 1))
                if u >= 4:
                    ve.tensor_scalar(small[:, s + 2:s + 3], small[:, s:s + 1], small[:, s + 1:s + 2], -1.0, ALU.max, ALU.mult
                                     ).then_inc(shift_ready, 1)
                else:
                    ve.tensor_scalar(small[:, s + 2:s + 3], small[:, s + 1:s + 2], -1.0, None, ALU.mult).then_inc(shift_ready, 1)

            def invert_sum(m, u):
                s = 40 + 8 * (u % 2)
                ve.wait_ge(exp_done, START + m * UNITS + (u + 1))
                ve.reciprocal(small[:, s + 4:s + 5], small[:, s + 3:s + 4]).then_inc(prob_step, 1)

            def normalise(m, u):
                s = 40 + 8 * (u % 2)
                n = keys(place(m, u)[0])[0] * P
                ve.wait_ge(prob_step, m * UNITS + (u + 1))
                ve.tensor_scalar(probs[:, u % PROBS, 0:n], probs[:, u % PROBS, 0:n], small[:, s + 4:s + 5], None, ALU.mult
                                 ).then_inc(probs_ready, 1)

            def softmax(m, u, more=True):
                at_m, at_u = (m, u) if u < UNITS else (m + 1, u - UNITS)
                before = (m, u - 1) if u - 1 < UNITS else (m + 1, u - 1 - UNITS)
                if more:
                    maxima(at_m, at_u)
                if u >= 1:
                    invert_sum(*before)
                if more:
                    shift(at_m, at_u)
                if u >= 1:
                    normalise(*before)

            def copy_v(m, first, last):
                ve.tensor_copy(v_fix[:, first:last, :], vb_tok[:, first:last, bass.ds(m * P, P)] if type(m) is not int else
                               vb_tok[:, first:last, m * P:(m + 1) * P]).then_inc(v_fixed, 1)

            def heads(m, final):
                for s in range(UNITS):
                    u = s + AHEAD
                    if s % 2:
                        t = place(m, s)[0]
                        cols = slice(t * P, (t + 1) * P)
                        if final:
                            ve.wait_ge(yb_hi_ready, s // 2 + 1)
                            ve.tensor_tensor(p_lo[:, 7, cols], ps[:, 6, 0:P], p_hi[:, 7, cols].bitcast(F32), ALU.subtract
                                             ).then_inc(mix_last_ready, 1)
                        else:
                            ve.wait_ge(pv_done, START + m * UNITS + (s + 1))
                            ve.tensor_scalar(yb[:, m, cols], ps[:, 6, 0:P], 1.0, None, ALU.mult).then_inc(yb_taken, 1)
                    if not final and s in HALF_ENDS:
                        n = HALF_ENDS.index(s)
                        cols = slice(n % 2 * HALF, (n % 2 + 1) * HALF)
                        ve.wait_ge(half_done, m * 4 + (n + 1))
                        if n == 0:
                            ve.wait_ge(qk_fixed, m * 4 + 4)
                        if n < 2:
                            ve.scalar_tensor_tensor(out=q_next[:, cols], in0=ps[:, 7, :], scalar=float(HD) ** -0.5, in1=rstd[:, cols],
                                                    op0=ALU.mult, op1=ALU.mult).then_inc(half_taken, 1)
                        else:
                            ve.tensor_tensor(k_next[:, cols], ps[:, 7, :], rstd[:, cols], ALU.mult).then_inc(half_taken, 1)
                    if u <= UNITS or not final:
                        softmax(m, u, not final or u < UNITS)
                    if final and s % 2 and s // 2 < 7:
                        n = s // 2
                        ve.wait_ge(half_done, 12)
                        ve.wait_ge(ya_ready, 4)
                        ve.wait_ge(yb_taken, START + 3 * 8)
                        ve.tensor_copy(p_hi[:, n, :], au[:, 4 + n, :] if n < 4 else yb[:, n - 4, :]).then_inc(mix_hi_ready, 1)
                    if final:
                        continue
                    if s == 10:
                        ve.wait_ge(half_taken, START + m * 4 + 4)
                        ve.wait_ge(scores_done, m * UNITS + 14)
                        ve.tensor_copy(q_fix[:, 0:7 * P], q_next[:, 0:7 * P]).then_inc(qk_fixed, 1)
                        ve.tensor_copy(k_fix[:, 0:3 * P], k_next[:, 0:3 * P]).then_inc(qk_fixed, 1)
                    if s == 11:
                        ve.wait_ge(scores_done, m * UNITS + 16)
                        ve.tensor_copy(q_fix[:, 7 * P:T], q_next[:, 7 * P:T]).then_inc(qk_fixed, 1)
                        ve.tensor_copy(k_fix[:, 3 * P:T], k_next[:, 3 * P:T]).then_inc(qk_fixed, 1)
                        ve.wait_ge(near_ready, m * UNITS + 16)
                        ve.tensor_copy(skew_fix[:, :, :], skew[:, bass.ds(m * 2 + 2, 2), :]).then_inc(skew_fixed, 1)
                        ve.wait_ge(skew_fixed, m + 2)
                    if s == 14:
                        ve.wait_ge(pv_done, START + m * UNITS + 14)
                        copy_v(m + 1, 0, 3)
                    if s == 15:
                        ve.wait_ge(pv_done, START + m * UNITS + 16)
                        copy_v(m + 1, 3, 8)

            for u in range(AHEAD):
                softmax(0, u)
                if u == 1:
                    ve.wait_ge(vb_copied, 8)
                    copy_v(0, 0, 3)
                    copy_v(0, 3, 8)
            with ve.Fori(0, 3) as m:
                heads(m, False)
            heads(3, True)

            def down(k, name, bias=None):
                def work(i, j, c):
                    n = i * QUAD + j
                    ve.wait_ge(gemm_done, c + 1)
                    if bias is None:
                        ve.tensor_tensor(xt[:, n, :], pair(j), xt[:, n, :], ALU.add).then_inc(evacuated, 1)
                    else:
                        ve.scalar_tensor_tensor(out=xt[:, n, :], in0=pair(j), scalar=gain(bias, n), in1=xt[:, n, :],
                                                op0=ALU.add, op1=ALU.add).then_inc(evacuated, 1)
                    if k is not None:
                        ve.wait_ge(evacuated, c + 1)
                        if k < 4:
                            low_part(k, n, gain(name, n + (8 if name == "g_mix" or k == 3 else 0)), q_hi, q_lo)
                        add_square(k, n)
                return work

            ve.sem_inc(evacuated, IN_CHUNKS - PRE_CHUNKS)
            clear_sum(1)
            quads(c_out, 2, down(1, "g_ffn"))
            for layer in range(2):
                if layer == 1:
                    invert(2)
                    for z in z_pad:
                        ve.memset(z[:, 0:PAD], 0.0).then_inc(z_cleared, 1)
                    ve.wait_ge(z_cleared, 2)

                    def make_z(n, parity):
                        ve.wait_ge(sigmoid_done, n + 1)
                        ve.scalar_tensor_tensor(out=z_pad[parity][:, PAD:PAD + T], in0=gate[:, :], scalar=gain("c_b1", n), in1=act[:, :],
                                                op0=ALU.add, op1=ALU.mult).then_inc(z_ready, 1)

                    def take(n, j, again=True):
                        if j == 0 and (type(n) is not int or n > 0):
                            ve.wait_ge(z_ready, START + n)
                        evacuate(n * 2 + (c_conv + j), j, (gate, up)[j][:, :])

                    take(0, 0)
                    take(0, 1)
                    make_z(0, 0)

                    def conv_step(i):
                        for e in range(2):
                            n = i * 2 + e
                            peeled = type(n) is int
                            first = peeled and n == 0
                            taps = VE_TAPS[n if peeled else 2]
                            done = START + taps_before(n)
                            ahead = {}
                            if first:
                                ahead = {6: lambda: take(1, 0), 15: lambda: (take(1, 1), make_z(1, 1)),
                                         20: lambda: take(2, 0), 29: lambda: take(2, 1)}
                            elif not peeled or n + 2 < NT:
                                ahead = {4: lambda: take(n + 2, 0), taps - 4: lambda: take(n + 2, 1)}
                            sums, z = (pair(2), pair(3)), z_pad[e]
                            for k in range(taps):
                                weight = chan[:, bass.ds(n * CONV_W + (COLS["c_dw"] + k), 1)]
                                total, taken = sums[k % 2], z[:, k:k + T]
                                ve.wait_ge(tap_done, done + max(k - 1, 0))
                                if k == 0:
                                    ve.wait_ge(z_ready, START + n + 1)
                                if k == 0 and first:
                                    ve.tensor_scalar(total, taken, weight, gain("c_bdw", n), ALU.mult, ALU.add).then_inc(tap_done, 1)
                                elif k == 0:
                                    ve.wait_ge(tap_folded, folded_before(n + 1))
                                    ve.scalar_tensor_tensor(out=total, in0=taken, scalar=weight, in1=pool_sum[e][:, :], op0=ALU.mult,
                                                            op1=ALU.add).then_inc(tap_done, 1)
                                elif k == 1 and peeled and PE_TAPS[n]:
                                    ve.wait_ge(pe_taps_done, n - (NT - 3))
                                    ve.scalar_tensor_tensor(out=total, in0=taken, scalar=weight, in1=pair(e), op0=ALU.mult,
                                                            op1=ALU.add).then_inc(tap_done, 1)
                                elif k == 1:
                                    ve.tensor_scalar(total, taken, weight, None, ALU.mult).then_inc(tap_done, 1)
                                else:
                                    leaves = k % 2 and k + 2 >= taps
                                    ve.scalar_tensor_tensor(out=y[:, n, :] if leaves else total, in0=taken, scalar=weight, in1=total, op0=ALU.mult,
                                                            op1=ALU.add).then_inc(tap_done, 1)
                                if k in ahead:
                                    ahead[k]()
                            ve.wait_ge(tap_done, done + taps)
                            ve.tensor_tensor(y[:, n, :], sums[0], y[:, n, :], ALU.add).then_inc(tap_done, 1)
                            if not peeled or n + 2 < NT:
                                ve.wait_ge(tap_done, done + taps)
                                make_z(n + 2, e)

                    conv_pairs(conv_step, ve)
                    ve.wait_ge(cln_sums, 1)
                    for n in range(NT):
                        ve.scalar_tensor_tensor(out=y[:, n, :], in0=pair(0), scalar=-1.0 / D, in1=y[:, n, :], op0=ALU.mult, op1=ALU.add
                                                ).then_inc(cln_centred, 1)
                    for n, (into, tile) in enumerate(((4, 5), (6, 7), (4, 6), (4, 0))):
                        ve.wait_ge(cln_step, max(tile, into) + 1)
                        if n >= 2:
                            ve.wait_ge(cln_added, n)
                        if tile == 0:
                            ve.wait_ge(cln_added_pool, NT // 2 - 1)
                        ve.tensor_tensor(centred_sq[:, into, :], centred_sq[:, into, :], centred_sq[:, tile, :], ALU.add
                                         ).then_inc(cln_added, 1)
                    invert_columns(0)

                    def conv_low(n):
                        ve.wait_ge(s_hi_ready, n + 1)
                        ve.tensor_tensor(p_lo[:, n, :], silus[n % 4][:, :], p_hi[:, n, :].bitcast(F32), ALU.subtract).then_inc(s_even_ready, 1)

                    for n in range(NT):
                        if n >= 3 and n % 2:
                            conv_low(n - 3)
                        if n >= 4 and n % 2:
                            ve.wait_ge(s_odd_ready, (n - 4) // 2 + 1)
                        elif n >= 4:
                            ve.wait_ge(s_even_ready, (n - 4) // 2 + 1)
                        ve.tensor_tensor(silus[n % 4][:, :], y[:, n, :], pair(2), ALU.mult).then_inc(cln_scaled, 1)
                    conv_low(NT - 2)
                    ve.wait_ge(s_odd_ready, NT // 2)
                    clear_sum(3)
                    quads(c_proj, 2, down(3, "g_ffn", bias="c_b2"))
                norm = 1 + 2 * layer
                invert(norm)
                clear_sum(2 + 2 * layer)
                for n, (c_up, c_dn, g, f0) in enumerate(ffn_at[layer]):
                    base = FT * layer + f0

                    def inner(i, j, c):
                        f = i * 2 + (base + j // 2)
                        if j % 2 == 0:
                            evacuate(c, j, gate[:, :])
                            return
                        ve.wait_ge(act_ready, START + f)
                        evacuate(c, j, up[:, :])
                        ve.wait_ge(silu_done, f + 1)
                        ve.wait_ge(evacuated, c + 1)
                        ve.tensor_tensor(up[:, :], up[:, :], act[:, :], ALU.mult).then_inc(product_ready, 1)
                        ve.wait_ge(act_hi_ready, f + 1)
                        k = i * 2 + j // 2
                        ve.tensor_tensor(p_lo[:, k, :], up[:, :], p_hi[:, k, :].bitcast(F32), ALU.subtract).then_inc(act_ready, 1)
                    quads(c_up, 2 * g // QUAD, inner)
                    last = n == len(GROUPS) - 1
                    quads(c_dn, 2, down(2 + 2 * layer if last else None, "g_mix"))
            invert_columns(1)
            for n in range(NT):
                ve.scalar_tensor_tensor(out=o_fin[:, n, :], in0=pair(2), scalar=gain("g_final", n), in1=xt[:, n, :],
                                        op0=ALU.mult, op1=ALU.mult).then_inc(out_ready, 1)


def kernel(x, w_in, w_out, a_ln_g, a_ln_b, a_ws, a_bs, b_rel, c_w1, c_b1, c_dw, c_bdw, c_ln_g, c_ln_b, c_w2, c_b2,
           g_mix, g_ffn, f_wg, f_wu, f_wd, g_final):
    import numpy as np
    import concourse.bacc as bacc
    from concourse import mybir as mb
    from concourse.bass_utils import run_bass_kernel_spmd

    def by_chunk(w):
        w = np.asarray(w)
        k, n = w.shape
        return w.reshape(k // P, P, n // P, P).transpose(2, 1, 0, 3).reshape(n // P, P, k)

    def by_partition(v):
        v = np.asarray(v)
        return v.reshape(-1, P).T

    wi = by_chunk(w_in[0])
    order = [4, 5, 6, 7, 0, 1, 2, 3, 16, 17, 18, 19, 8, 12, 9, 13, 10, 14, 11, 15]
    c1 = by_chunk(c_w1[0])
    rel = np.asarray(b_rel)[0][:, ::-1]
    ext = np.concatenate([np.broadcast_to(rel[:, :1], (HEADS, P - 1)), rel[:, :EXT - P + 1]], axis=1)
    dw = np.asarray(c_dw)[0].T.reshape(NT, P, CONV_W).transpose(1, 0, 2).reshape(P, NT * CONV_W)
    arrays = {
        "x": np.asarray(x)[0].T.reshape(NT, P, T),
        "w_in": wi[order],
        "w_out": by_chunk(w_out[0]),
        "w_ws": np.asarray(a_ws)[0].transpose(2, 0, 1),
        "b_bs": np.asarray(a_bs)[0],
        "ln_g": np.asarray(a_ln_g),
        "ln_b": np.asarray(a_ln_b),
        "rel_ext": ext,
        "rel_far": rel[:, :1].reshape(1, HEADS),
        "per_channel": np.concatenate([by_partition(v) for v in (g_mix, g_ffn, g_final, c_b1, c_bdw, c_ln_g, c_ln_b, c_b2)] + [dw], axis=1),
        "w_c1": np.stack([c1[:NT], c1[NT:]], axis=1).reshape(2 * NT, P, D),
        "w_c2": by_chunk(c_w2[0]),
        "w_gu": np.stack([np.stack([by_chunk(f_wg[n]), by_chunk(f_wu[n])], axis=1).reshape(2 * FT, P, D) for n in range(2)]),
        "w_dn": np.stack([by_chunk(f_wd[n]) for n in range(2)]),
    }
    arrays = {k: np.ascontiguousarray(v) for k, v in arrays.items()}
    nc = bacc.Bacc("TRN2", target_bir_lowering=False, num_devices=1, dynamic_dma_scratch_size=DMA_RING)
    args = {k: nc.dram_tensor(f"in_{k}", v.shape, mb.dt.from_np(v.dtype), kind="ExternalInput").ap() for k, v in arrays.items()}
    args["out"] = nc.dram_tensor("out", (NT, P, T), mb.dt.float32, kind="ExternalOutput").ap()
    build(nc, **args)
    r = run_bass_kernel_spmd(nc, [{f"in_{k}": v for k, v in arrays.items()}], core_ids=[0])
    return np.ascontiguousarray(r.results[0]["out"].reshape(D, T).T).reshape(1, T, D)
```
